# Optimizing a Trainium2 kernel written in Bass

```python
import jax, jax.numpy as jnp
from jax import lax
import numpy as np

D_MODEL = 1024
BATCH = 1
SEQ = 512
DEPTH = 1

HEAD_DIM = 64
SWA_Q_HEADS = 8
SWA_KV_HEADS = 2
SWA_WINDOW = 128
FOX_HEADS = 8
BLOCK = 128
ROPE_THETA = 10000.0
N_EXPERTS = 32
TOP_K = 4
D_FF_EXPERT = D_MODEL
SWIGLU_LIMIT = 7.0
SWIGLU_ALPHA = 1.702
EPS = 1e-6
NEG = -1e30
ATTN_SCALE = HEAD_DIM ** -0.5

SWA_Q_W = SWA_Q_HEADS * HEAD_DIM
SWA_KV_W = SWA_KV_HEADS * HEAD_DIM
FOX_W = FOX_HEADS * HEAD_DIM
IN_SPLITS = (SWA_Q_W, SWA_KV_W, SWA_KV_W, FOX_W, FOX_W, FOX_W, FOX_HEADS, 2 * D_MODEL)
IN_W = SWA_Q_W + 2 * SWA_KV_W + 3 * FOX_W + FOX_HEADS + 2 * D_MODEL

kernel_name = "hybrid_swa_sink_fox_moe_block"

def rms_norm(x, g):
    xf = x.astype(jnp.float32)
    y = xf * lax.rsqrt(jnp.mean(xf * xf, axis=-1, keepdims=True) + EPS)
    return (y * g.astype(jnp.float32)).astype(x.dtype)

def rope(x, positions):
    half = HEAD_DIM // 2
    inv = ROPE_THETA ** (-jnp.arange(half, dtype=jnp.float32) / half)
    ang = positions.astype(jnp.float32)[..., None] * inv
    cos = jnp.cos(ang)[:, :, None, :]
    sin = jnp.sin(ang)[:, :, None, :]
    xf = x.astype(jnp.float32)
    x1, x2 = xf[..., :half], xf[..., half:]
    return jnp.concatenate([x1 * cos - x2 * sin, x2 * cos + x1 * sin], axis=-1).astype(x.dtype)

def split_cols(p):
    idx, acc = [], 0
    for w in IN_SPLITS[:-1]:
        acc += w
        idx.append(acc)
    return jnp.split(p, idx, axis=-1)

def swa_sink_attention(q, k, v, sinks):
    B, S = q.shape[0], q.shape[1]
    nb = S // BLOCK
    G = SWA_Q_HEADS // SWA_KV_HEADS
    qb = q.reshape(B, nb, BLOCK, SWA_KV_HEADS, G, HEAD_DIM)
    kb = k.reshape(B, nb, BLOCK, SWA_KV_HEADS, HEAD_DIM)
    vb = v.reshape(B, nb, BLOCK, SWA_KV_HEADS, HEAD_DIM)

    def with_prev(t):
        prev = jnp.pad(t[:, :-1], ((0, 0), (1, 0), (0, 0), (0, 0), (0, 0)))
        return jnp.concatenate([prev, t], axis=2)

    kk, vv = with_prev(kb), with_prev(vb)
    s = jnp.einsum('bnqhgd,bnkhd->bnhgqk', qb, kk).astype(jnp.float32) * ATTN_SCALE
    qi = jnp.arange(BLOCK)[:, None]
    kj = jnp.arange(2 * BLOCK)[None, :]
    delta = qi + BLOCK - kj
    blk = jnp.arange(nb)[:, None, None]
    valid = (delta >= 0) & (delta < SWA_WINDOW) & (blk * BLOCK + kj - BLOCK >= 0)
    s = jnp.where(valid[None, :, None, None], s, NEG)
    sink = sinks.astype(jnp.float32).reshape(1, 1, SWA_KV_HEADS, G, 1, 1)
    m = jnp.maximum(jnp.max(s, axis=-1, keepdims=True), sink)
    p = jnp.exp(s - m)
    p = p / (jnp.sum(p, axis=-1, keepdims=True) + jnp.exp(sink - m))
    o = jnp.einsum('bnhgqk,bnkhd->bnqhgd', p.astype(v.dtype), vv)
    return o.reshape(B, S, SWA_Q_W)

def forgetting_attention(q, k, v, log_f):
    B, S = q.shape[0], q.shape[1]
    nb = S // BLOCK
    c = jnp.cumsum(log_f, axis=1).transpose(0, 2, 1)
    qb = q.reshape(B, nb, BLOCK, FOX_HEADS, HEAD_DIM).transpose(1, 0, 2, 3, 4)
    cq = c.reshape(B, FOX_HEADS, nb, BLOCK).transpose(2, 0, 1, 3)
    k_pos = jnp.arange(S)

    def block(args):
        q_blk, c_blk, n = args
        s = jnp.einsum('bqhd,bkhd->bhqk', q_blk, k).astype(jnp.float32) * ATTN_SCALE
        s = s + c_blk[..., None] - c[:, :, None, :]
        q_pos = n * BLOCK + jnp.arange(BLOCK)
        s = jnp.where((k_pos[None, :] <= q_pos[:, None])[None, None], s, NEG)
        p = jax.nn.softmax(s, axis=-1).astype(v.dtype)
        return jnp.einsum('bhqk,bkhd->bqhd', p, v)

    o = lax.map(block, (qb, cq, jnp.arange(nb)))
    return o.transpose(1, 0, 2, 3, 4).reshape(B, S, FOX_W)

def moe_ffn(h, w_router, b_router, w_gate_up, b_gate_up, w_down, b_down):
    B, S, D = h.shape
    N = B * S
    t = h.reshape(N, D)
    logits = (t @ w_router).astype(jnp.float32) + b_router.astype(jnp.float32)
    top_val, top_idx = lax.top_k(logits, TOP_K)
    gate = jax.nn.softmax(top_val, axis=-1)
    e_flat = top_idx.reshape(-1).astype(jnp.int32)
    tok_flat = jnp.repeat(jnp.arange(N, dtype=jnp.int32), TOP_K)
    w_flat = gate.reshape(-1)
    order = jnp.argsort(e_flat)
    e_sorted = e_flat[order]
    counts = jnp.zeros((N_EXPERTS,), jnp.int32).at[e_flat].add(1)
    padded = (counts + BLOCK - 1) // BLOCK * BLOCK
    pad_end = jnp.cumsum(padded)
    pad_start = pad_end - padded
    grp_start = jnp.cumsum(counts) - counts
    rank = jnp.arange(N * TOP_K, dtype=jnp.int32) - grp_start[e_sorted]
    dest = pad_start[e_sorted] + rank
    cap = N * TOP_K + N_EXPERTS * BLOCK
    n_blk = cap // BLOCK
    row_tok = jnp.full((cap,), N, jnp.int32).at[dest].set(tok_flat[order])
    row_w = jnp.zeros((cap,), jnp.float32).at[dest].set(w_flat[order])
    blk_expert = jnp.minimum(jnp.searchsorted(pad_end, jnp.arange(n_blk, dtype=jnp.int32) * BLOCK, side='right'),
                             N_EXPERTS - 1).astype(jnp.int32)
    t_pad = jnp.concatenate([t, jnp.zeros((1, D), t.dtype)], axis=0)
    xin = t_pad[row_tok].reshape(n_blk, BLOCK, D)

    def expert_block(args):
        xb, e = args
        gu = xb @ w_gate_up[e] + b_gate_up[e]
        g, u = gu[:, :D_FF_EXPERT], gu[:, D_FF_EXPERT:]
        g = jnp.minimum(g, SWIGLU_LIMIT)
        u = jnp.clip(u, -SWIGLU_LIMIT, SWIGLU_LIMIT)
        a = (u + 1.0) * (g * jax.nn.sigmoid(SWIGLU_ALPHA * g))
        return a @ w_down[e] + b_down[e]

    yb = lax.map(expert_block, (xin, blk_expert)).reshape(cap, D)
    y = jax.ops.segment_sum(yb * row_w[:, None].astype(yb.dtype), row_tok, num_segments=N + 1)[:N]
    return y.reshape(B, S, D)

def hybrid_layer(x, positions, norm1_g, w_in, b_forget, b_gate, q_norm_swa, k_norm_swa, sinks,
                 q_norm_fox, k_norm_fox, w_o_swa, w_o_fox, w_out, norm2_g, w_router, b_router,
                 w_gate_up, b_gate_up, w_down, b_down):
    B, S, D = x.shape
    h = rms_norm(x, norm1_g)
    proj = h @ w_in
    qa, ka, va, qf, kf, vf, fl, gl = split_cols(proj)
    qa = rope(rms_norm(qa.reshape(B, S, SWA_Q_HEADS, HEAD_DIM), q_norm_swa), positions)
    ka = rope(rms_norm(ka.reshape(B, S, SWA_KV_HEADS, HEAD_DIM), k_norm_swa), positions)
    va = va.reshape(B, S, SWA_KV_HEADS, HEAD_DIM)
    out_a = swa_sink_attention(qa, ka, va, sinks)
    qf = rms_norm(qf.reshape(B, S, FOX_HEADS, HEAD_DIM), q_norm_fox)
    kf = rms_norm(kf.reshape(B, S, FOX_HEADS, HEAD_DIM), k_norm_fox)
    vf = vf.reshape(B, S, FOX_HEADS, HEAD_DIM)
    log_f = jax.nn.log_sigmoid((fl + b_forget).astype(jnp.float32))
    out_b = forgetting_attention(qf, kf, vf, log_f)
    gates = jax.nn.sigmoid(gl + b_gate)
    g_a, g_b = gates[..., :D_MODEL], gates[..., D_MODEL:]
    merged = g_a * (out_a @ w_o_swa) + g_b * (out_b @ w_o_fox)
    x = x + merged @ w_out
    h2 = rms_norm(x, norm2_g)
    return x + moe_ffn(h2, w_router, b_router, w_gate_up, b_gate_up, w_down, b_down)

def setup_inputs(seed: int = 0) -> dict:
    key = jax.random.key(seed)
    ks = jax.random.split(key, 24)
    f32 = jnp.float32

    def nrm(k, shape, scale):
        return jax.random.normal(k, shape, f32) * scale

    L = DEPTH
    return {
        "x": nrm(ks[0], (BATCH, SEQ, D_MODEL), 1.0),
        "positions": (jnp.arange(SEQ, dtype=jnp.int32)[None, :]
                      + jax.random.randint(ks[1], (BATCH, 1), 0, 4096, dtype=jnp.int32)),
        "norm1_g": 1.0 + nrm(ks[2], (L, D_MODEL), 0.02),
        "w_in": nrm(ks[3], (L, D_MODEL, IN_W), D_MODEL ** -0.5),
        "b_forget": 3.0 + nrm(ks[4], (L, FOX_HEADS), 0.5),
        "b_gate": nrm(ks[5], (L, 2 * D_MODEL), 0.02),
        "q_norm_swa": 1.0 + nrm(ks[6], (L, HEAD_DIM), 0.02),
        "k_norm_swa": 1.0 + nrm(ks[7], (L, HEAD_DIM), 0.02),
        "sinks": nrm(ks[8], (L, SWA_Q_HEADS), 0.5),
        "q_norm_fox": 1.0 + nrm(ks[9], (L, HEAD_DIM), 0.02),
        "k_norm_fox": 1.0 + nrm(ks[10], (L, HEAD_DIM), 0.02),
        "w_o_swa": nrm(ks[11], (L, SWA_Q_W, D_MODEL), SWA_Q_W ** -0.5),
        "w_o_fox": nrm(ks[12], (L, FOX_W, D_MODEL), FOX_W ** -0.5),
        "w_out": nrm(ks[13], (L, D_MODEL, D_MODEL), D_MODEL ** -0.5),
        "norm2_g": 1.0 + nrm(ks[14], (L, D_MODEL), 0.02),
        "w_router": nrm(ks[15], (L, D_MODEL, N_EXPERTS), D_MODEL ** -0.5),
        "b_router": nrm(ks[16], (L, N_EXPERTS), 0.01),
        "w_gate_up": nrm(ks[17], (L, N_EXPERTS, D_MODEL, 2 * D_FF_EXPERT), D_MODEL ** -0.5),
        "b_gate_up": nrm(ks[18], (L, N_EXPERTS, 2 * D_FF_EXPERT), 0.01),
        "w_down": nrm(ks[19], (L, N_EXPERTS, D_FF_EXPERT, D_MODEL), D_FF_EXPERT ** -0.5),
        "b_down": nrm(ks[20], (L, N_EXPERTS, D_MODEL), 0.01),
    }

def reference(x, positions, norm1_g, w_in, b_forget, b_gate, q_norm_swa, k_norm_swa, sinks,
              q_norm_fox, k_norm_fox, w_o_swa, w_o_fox, w_out, norm2_g, w_router, b_router,
              w_gate_up, b_gate_up, w_down, b_down):
    for l in range(DEPTH):
        x = hybrid_layer(x, positions, norm1_g[l], w_in[l], b_forget[l], b_gate[l],
                         q_norm_swa[l], k_norm_swa[l], sinks[l], q_norm_fox[l], k_norm_fox[l],
                         w_o_swa[l], w_o_fox[l], w_out[l], norm2_g[l], w_router[l], b_router[l],
                         w_gate_up[l], b_gate_up[l], w_down[l], b_down[l])
    return x


_drawn_inputs = setup_inputs


def setup_inputs(seed=0):
    import zlib

    import numpy as np

    out = dict(_drawn_inputs(seed))
    spreads = {}
    factors = {'b_gate': 4.408,
     'q_norm_swa': 3.457,
     'k_norm_swa': 3.969,
     'sinks': 31.057,
     'k_norm_fox': 3.563,
     'b_gate_up': 8.0,
     'b_down': 8.0}
    for name, (base, spread) in spreads.items():
        noise = np.random.default_rng([zlib.crc32(name.encode()), seed]).standard_normal(out[name].shape)
        drawn = base * np.exp(spread * noise) if base else spread * noise
        out[name] = __import__('jax').numpy.asarray(drawn.astype(out[name].dtype))
    for name, factor in factors.items():
        out[name] = (out[name] * factor).astype(out[name].dtype)
    return out
```

```python
from contextlib import ExitStack

import numpy as np

import concourse.bass as bass
from concourse import mybir

F32 = mybir.dt.float32
F32R = mybir.dt.float32r
BF16 = mybir.dt.bfloat16
I32 = mybir.dt.int32
ALU = mybir.AluOpType
ACT = mybir.ActivationFunctionType
AX = mybir.AxisListType

P = 128
HD = 64
ROPE_THETA = 10000.0
TOP_K = 4
LIMIT = 7.0
ALPHA = 1.702
EPS = 1e-6
NEG = -1e30
SCALE = HD ** -0.5
GW = 256
SLOTS = 96
MAGIC = 12582912.0
TWO_PI = 2.0 * np.pi
C1 = 6.28125
C2 = float(np.float32(np.floor((TWO_PI - C1) * 2 ** 21) / 2 ** 21))
C3 = float(np.float32(TWO_PI - C1 - C2))


def bc(ap, axis, n):
    new = ap.unsqueeze(axis)
    shape = list(new.shape)
    shape[axis] = n
    return new.broadcast_to(shape)


def hybrid_block(nc, x, positions, norm1_g, w_in, b_forget, b_gate, q_norm_swa, k_norm_swa, sinks,
                 q_norm_fox, k_norm_fox, w_o_swa, w_o_fox, w_out, norm2_g, w_router, b_router,
                 w_gate_up, b_gate_up, w_down, b_down, out):
    T, D = x.shape[1:]
    NB, KD = T // P, D // P
    HF = b_forget.shape[1]
    HQ = sinks.shape[1]
    QW, FW = HQ * HD, HF * HD
    KV = (w_in.shape[2] - QW - 3 * FW - HF - 2 * D) // (2 * HD)
    KVW = KV * HD
    QKV = QW + 2 * KVW + 3 * FW
    E, F = w_gate_up.shape[1], w_down.shape[2]
    F2 = 2 * F
    assert (NB, KD, HQ, HF, KV, E, F, QKV) == (4, 8, 8, 8, 2, 32, 1024, 2304)
    KA, VA, QF = QW, QW + KVW, QW + 2 * KVW
    KF, VF = QF + FW, QF + 2 * FW
    FL, GATE = QKV, QKV + HF
    SWA_H, FOX_H = HQ + KV, 2 * HF

    N_QKV, N_GATE, N_O, N_OUT = QKV // GW, 2 * D // GW, D // GW, D // GW
    G_GATE, G_O = N_QKV, N_QKV + N_GATE
    G_OUT = G_O + N_O
    G_END = G_OUT + N_OUT

    MAX_EXTRA = T * TOP_K // SLOTS
    LEVELS = -(-T // SLOTS) - 1
    ITEMS = E + MAX_EXTRA + 1
    N_AT, LAST_AT = 63, 62

    stage_waits = []
    total = [0, 0]
    for g in range(G_END):
        total[g % 2] += 32 if G_O <= g < G_OUT else 16
        stage_waits.append(total[g % 2])

    with ExitStack() as ctx:
        base = (nc.sbuf_base + 63) // 64 * 64

        class Region:
            top = base

            def __init__(self, size):
                self.start, self.end = Region.top, Region.top + size
                self.at = self.start
                Region.top = self.end
                assert self.end <= nc.sbuf_usable_end, (self.end, nc.sbuf_usable_end)

            def rewind(self, offset=0):
                self.at = self.start + offset

            def put(self, name, shape, dt=F32):
                size = int(np.prod(shape[1:])) * (2 if dt == BF16 else 4)
                t = nc.alloc_sbuf_tensor_at(name, shape, dt, offset=self.at)
                self.at += (size + 31) // 32 * 32
                assert self.at <= self.end, (name, self.at - self.end)
                return t

        K = 1024
        stage, hold = Region(48 * K), Region(48 * K)
        xreg, r1, r2, work, const = Region(16 * K), Region(32 * K), Region(36 * K), Region(10 * K), Region(17 * K)

        st_w = stage.put("st_w", [P, 2, KD, GW])
        st_h = stage.put("st_h", [P, 2, KD, GW], F32R)
        st_l = stage.put("st_l", [P, 2, KD, GW], F32R)
        stage.rewind()
        gu_tail = stage.put("gu_tail", [P, 2, F2])
        wdn = stage.put("wdn", [P, 4, 2, D])
        stage.rewind(16 * K)
        wdn_l = stage.put("wdn_l", [P, 4, 2, D], F32R)
        gates_T = hold.put("gates_T", [P, 2 * KD, T])
        o_tok = hold.put("o_tok", [P, NB, QW + FW])
        hold.rewind()
        gu_head = hold.put("gu_head", [P, 6, F2])
        hold.rewind()
        hn_tok = hold.put("hn_tok", [P, NB, D])
        bgu_rows = hold.put("bgu_rows", [E, F2])
        vec_rows = hold.put("vec_rows", [32, P])
        hold.rewind(32 * K)
        k_dup = hold.put("k_dup", [P, NB, KV, 2, HD])
        sq = hold.put("sq", [P, (SWA_H + FOX_H) * HD])
        rot = hold.put("rot", [P, 2, SWA_H, HD])
        x_tok = xreg.put("x_tok", [P, NB, D])
        hT_h = r1.put("hT_h", [P, KD, T], F32R)
        hT_l = r1.put("hT_l", [P, KD, T], F32R)
        r1.rewind()
        qaT = r1.put("qaT", [P, HQ // 2, T])
        kaT = r1.put("kaT", [P, KV, T])
        qfT = r1.put("qfT", [P, HF // 2, T])
        kfT = r1.put("kfT", [P, HF // 2, T])
        r1.rewind()
        oT_h = r1.put("oT_h", [P, KD, T], F32R)
        oT_l = r1.put("oT_l", [P, KD, T], F32R)
        r1.rewind()
        h2T = r1.put("h2T", [P, KD, T])
        h2n = r1.put("h2n", [P, NB, D])
        tok = r2.put("tok", [P, NB, QKV])
        r2.rewind()
        mT_h = r2.put("mT_h", [P, KD, T], F32R)
        mT_l = r2.put("mT_l", [P, KD, T], F32R)
        r2.rewind()
        xg = r2.put("xg", [SLOTS, D])
        xT = r2.put("xT", [P, KD, SLOTS])
        act_g = r2.put("act_g", [P, KD, SLOTS])
        act_u = r2.put("act_u", [P, KD, SLOTS])
        act_s = r2.put("act_s", [P, KD, SLOTS])
        aT = r2.put("aT", [P, KD, SLOTS])
        r2.at -= KD * SLOTS * 4
        aT_l = r2.put("aT_l", [P, KD, SLOTS], F32R)
        ysb = r2.put("ysb", [SLOTS, D])
        sel = r2.put("sel", [P, NB, SLOTS])
        zero_rows = r2.put("zero_rows", [SLOTS, D])
        c_hi = work.put("c_hi", [P, T], F32R)
        lf = work.put("lf", [P, NB, P])
        ang = work.put("ang", [P, NB, HD // 2])
        ang_k = work.put("ang_k", [P, NB, HD // 2])
        sin_t = work.put("sin_t", [P, NB, HD // 2])
        cos_t = work.put("cos_t", [P, NB, HD // 2])
        rope_c = work.put("rope_c", [P, 2, NB, HD])
        rope_s = work.put("rope_s", [P, 2, NB, HD])
        work.rewind()
        p_sb = work.put("p_sb", [P, 3, T])
        pT_sb = work.put("pT_sb", [P, 2, T])
        work.rewind()
        merge_t = work.put("merge_t", [P, 2, T])
        merge_s = work.put("merge_s", [P, 2, T])
        work.rewind()
        b_dn = work.put("b_dn", [P, D])
        gateT = work.put("gateT", [P, P])
        lg = work.put("lg", [P, NB, E])
        r_gt = work.put("r_gt", [P, NB, E])
        r_eq = work.put("r_eq", [P, NB, E])
        r_in = work.put("r_in", [P, NB, E])
        r_ex = work.put("r_ex", [P, NB, E])
        aT_h = work.put("aT_h", [P, KD, SLOTS], F32R)
        HN = SWA_H + FOX_H
        ident = const.put("ident", [P, P])
        ident_b = const.put("ident_b", [P, P], BF16)
        mask_b = const.put("mask_b", [P, 2, P], BF16)
        upto = const.put("upto", [P, T])
        before_b = const.put("before_b", [P, P], BF16)
        ones_b = const.put("ones_b", [P, P], BF16)
        iota_i = const.put("iota_i", [P, P], I32)
        iota_f = const.put("iota_f", [P, P])
        tok_i = const.put("tok_i", [P, NB], I32)
        tok_f = const.put("tok_f", [P, NB])
        spare = const.put("spare", [P, 1])
        zeros = const.put("zeros", [P, ITEMS])
        inv = const.put("inv", [P, HD // 2])
        vcol = const.put("vcol", [P, 32])
        bgu = const.put("bgu", [P, E, 2 * KD])
        c_rows = const.put("c_rows", [P, T], F32R)
        c_pick = const.put("c_pick", [P, HF])
        c_pick_r = const.put("c_pick_r", [P, HF], F32R)
        ssq = const.put("ssq", [P, 2, NB])
        rstd = const.put("rstd", [P, 2, NB])
        hs_sum = const.put("hs_sum", [P, NB, HN])
        hs_r = const.put("hs_r", [P, NB, HN])
        minus_half = const.put("minus_half", [P, NB, HN])
        fl = const.put("fl", [P, NB, HF])
        fl_a = const.put("fl_a", [P, NB, HF])
        bf_bc = const.put("bf_bc", [P, HF])
        sink_bc = const.put("sink_bc", [P, HQ])
        sink8 = const.put("sink8", [P, HQ])
        brt = const.put("brt", [P, E])
        w_rt = const.put("w_rt", [P, KD, E])
        g_sw = const.put("g_sw", [P, 2, HD])
        g_fx = const.put("g_fx", [P, 2])
        pos_i = const.put("pos_i", [P, NB], I32)
        pos_f = const.put("pos_f", [P, NB])
        mx = const.put("mx", [P, 64])
        nb = const.put("nb", [P, 64])
        den = const.put("den", [P, 64])
        rden = const.put("rden", [P, 64])
        snk = const.put("snk", [P, HQ])
        wfl = const.put("wfl", [P, KD, HF])
        wfl_h = const.put("wfl_h", [P, KD, HF], F32R)
        wfl_l = const.put("wfl_l", [P, KD, HF], F32R)
        top8 = r2.put("top8", [P, NB, 8])
        need = r2.put("need", [P, NB])
        zsum = r2.put("zsum", [P, NB])
        sel_b = r2.put("sel_b", [P, NB, E], BF16)
        slot_tab = r2.put("slot_tab", [P, NB, ITEMS])
        row_tab = r2.put("row_tab", [P, NB, ITEMS, 2])
        cnt = r2.put("cnt", [P, E])
        ext = r2.put("ext", [P, E])
        ext_in = r2.put("ext_in", [P, E])
        ext_ex = r2.put("ext_ex", [P, E])
        item_e = r2.put("item_e", [P, MAX_EXTRA])
        item_b = r2.put("item_b", [P, MAX_EXTRA])
        items_f = r2.put("items_f", [1, 64])
        items = r2.put("items", [1, 64], I32)
        idx_g = r2.put("idx_g", [SLOTS, 1], I32)
        idx_s = r2.put("idx_s", [SLOTS, 1], I32)
        idx_all = r2.put("idx_all", [SLOTS, ITEMS], I32)
        gate_all = r2.put("gate_all", [SLOTS, ITEMS])
        r1.rewind()
        onehot = r1.put("onehot", [P, MAX_EXTRA, E])
        onehot_t = r1.put("onehot_t", [P, MAX_EXTRA, E])
        r1.rewind()
        wdn_h = r1.put("wdn_h", [P, 4, 2, D], F32R)

        ps = ctx.enter_context(nc.psum_tensor("ps", [P, 8, 512], F32))
        xT_ps_v = ps[:, 6:8, :].rearrange("p b (k s) -> p (b k) s", k=4)[:, :, 0:SLOTS]
        list_v = ps[0:SLOTS, 6, SLOTS:SLOTS + 2]
        gu_v = ps[:, 0:4, :].rearrange("p b (k s) -> p (b k) s", k=4)[:, :, 0:SLOTS]
        h2_dram = nc.dram_tensor("h2_dram", (T, D), F32, kind="Internal").ap()
        acc_dram = nc.dram_tensor("acc_dram", (T + SLOTS, D), F32, kind="Internal").ap()
        BIG = 8.0 * T

        x_v = x[0].rearrange("(c p) d -> p c d", p=P)
        w_in_v = w_in[0].rearrange("(k p) n -> p k n", p=P)
        w_oa_v = w_o_swa[0].rearrange("(k p) n -> p k n", p=P)
        w_ob_v = w_o_fox[0].rearrange("(k p) n -> p k n", p=P)
        w_out_v = w_out[0].rearrange("(k p) n -> p k n", p=P)
        w_gu_v = w_gate_up.rearrange("l e (k p) n -> (l e) k p n", p=P)
        w_dn_v = w_down.rearrange("l e (j k p) n -> (l e) j p k n", p=P, k=2)

        def sem(name):
            return ctx.enter_context(nc.semaphore(name))

        x_in = [sem(f"x_in{c}") for c in range(NB)]
        rows_in, small_in, wfl_in = sem("rows_in"), sem("small_in"), sem("wfl_in")
        stage_in = [sem("stage_in0"), sem("stage_in1")]
        b_dn_in = sem("b_dn_in")
        gu_in = [sem(f"gu_in{k}") for k in range(KD)]
        dn_in = [sem(f"dn_in{j}") for j in range(4)]
        pool_step, dve_step = sem("pool_step"), sem("dve_step")
        consts, ident_done, squared = sem("consts"), sem("ident_done"), sem("squared")
        var_ready, rstd_ready, hn_ready = sem("var_ready"), sem("rstd_ready"), sem("hn_ready")
        hT_ps, hT_hi, hT_ready = sem("hT_ps"), sem("hT_hi"), sem("hT_ready")
        rows_ps, vcol_ready, bgu_ready = sem("rows_ps"), sem("vcol_ready"), sem("bgu_ready")
        split_hi, split_lo = sem("split_hi"), sem("split_lo")
        group_done, group_out = sem("group_done"), sem("group_out")
        wfl_hi, wfl_ready, fl_ps = sem("wfl_hi"), sem("wfl_ready"), sem("fl_ps")
        fl_abs, fl_exp, fl_ln = sem("fl_abs"), sem("fl_exp"), sem("fl_ln")
        lf_ready, c_ps, c_hi_ready, c_ready = sem("lf_ready"), sem("c_ps"), sem("c_hi_ready"), sem("c_ready")
        heads_sq, sq_read, hs_var, hs_rstd = sem("heads_sq"), sem("sq_read"), sem("hs_var"), sem("hs_rstd")
        ang_ready, sin_ready, qk_ready = sem("ang_ready"), sem("sin_ready"), sem("qk_ready")
        qkT_ps, qkT_out = sem("qkT_ps"), [sem("qkT_out0"), sem("qkT_out1")]
        scores, maxed, shift, probs = sem("scores"), sem("maxed"), sem("shift"), sem("probs")
        pT_ps, pT_ready, pv_done = sem("pT_ps"), sem("pT_ready"), sem("pv_done")
        snk_in, snk_exp, o_out = sem("snk_in"), sem("snk_exp"), sem("o_out")
        oT_ps, oT_hi, oT_ready = sem("oT_ps"), sem("oT_hi"), sem("oT_ready")
        m_part, m_sum, m_hi, m_ready = sem("m_part"), sem("m_sum"), sem("m_hi"), sem("m_ready")
        x1_ready, h2_ready, h2_stored = sem("x1_ready"), sem("h2_ready"), sem("h2_stored")
        h2T_ps, h2T_out = sem("h2T_ps"), [sem("h2T_out0"), sem("h2T_out1")]
        logits_ps, r_shifted, r_exp, picked = sem("logits_ps"), sem("r_shifted"), sem("r_exp"), sem("picked")
        place_ps, gates_ready, gateT_ps, gateT_ready = (sem("place_ps"), sem("gates_ready"), sem("gateT_ps"),
                                                        sem("gateT_ready"))
        bdn_ps, bdn_out, acc_set = sem("bdn_ps"), sem("bdn_out"), sem("acc_set")
        items_ready, zero_ready = sem("items_ready"), sem("zero_ready")
        sel_ready, list_ps, idx_ready, xg_in = sem("sel_ready"), sem("list_ps"), sem("idx_ready"), sem("xg_in")
        xT_ps, xT_ready = sem("xT_ps"), sem("xT_ready")
        gu_used = [sem(f"gu_used{k}") for k in range(KD)]
        g_biased, gu_out, g_ready, u_ready = sem("g_biased"), sem("gu_out"), sem("g_ready"), sem("u_ready")
        sig_ready, gs_ready, a_whole = sem("sig_ready"), sem("gs_ready"), sem("a_whole")
        a_hi, a_ready = sem("a_hi"), sem("a_ready")
        dn_hi = [sem(f"dn_hi{j}") for j in range(4)]
        dn_lo = [sem(f"dn_lo{j}") for j in range(4)]
        dn_used = [sem(f"dn_used{j}") for j in range(4)]
        idx_s_ready, added, turn = sem("idx_s_ready"), sem("added"), sem("turn")
        y_ready, y_free = sem("y_ready"), sem("y_free")
        out_done = sem("out_done")

        def gu_chunk(k):
            return gu_head[:, k, :] if k < 6 else gu_tail[:, k - 6, :]

        units = [(c, b, h) for c in range(NB) for b in (0, 1) for h in range(8)]
        NU = len(units)
        QKT = [(s, j) for s in range(4) for j in range((HQ // 2, KV, HF // 2, HF // 2)[s])]

        def width(n):
            c, fox, _ = units[n]
            return (c + 1) * P if fox else min(c + 1, 2) * P

        block = ctx.enter_context(nc.Block())

        @block.sync
        def _(sp):
            for c in range(NB):
                sp.dma_start(x_tok[:, c, :], x_v[:, c, :]).then_inc(x_in[c], 16)

            for g in range(G_END):
                if g >= 2:
                    sp.wait_ge(split_lo, g - 1)
                dst, s = st_w[:, g % 2], stage_in[g % 2]
                if g < G_O:
                    c0 = g * GW if g < G_GATE else GATE + (g - G_GATE) * GW
                    sp.dma_start(dst, w_in_v[:, :, c0:c0 + GW]).then_inc(s, 16)
                elif g < G_OUT:
                    c0 = (g - G_O) * GW
                    sp.dma_start(dst[:, 0:4], w_oa_v[:, :, c0:c0 + GW]).then_inc(s, 16)
                    sp.dma_start(dst[:, 4:8], w_ob_v[:, :, c0:c0 + GW]).then_inc(s, 16)
                else:
                    c0 = (g - G_OUT) * GW
                    sp.dma_start(dst, w_out_v[:, :, c0:c0 + GW]).then_inc(s, 16)
                if g == 0:
                    sp.dma_start(wfl[:, :, :], w_in_v[:, :, FL:FL + HF]).then_inc(wfl_in, 16)

            def load_gu(e, k):
                src = w_gu_v[e, k] if isinstance(e, int) else w_gu_v[bass.ds(e, 1), k].rearrange("a p n -> (a p) n")
                sp.dma_start(gu_chunk(k), src).then_inc(gu_in[k], 16)

            def load_dn(e, j):
                src = w_dn_v[e, j] if isinstance(e, int) else w_dn_v[bass.ds(e, 1), j].rearrange("a p k n -> (a p) k n")
                sp.dma_start(wdn[:, j, :, :], src).then_inc(dn_in[j], 16)

            sp.wait_ge(m_sum, KD)
            for k in range(6):
                load_gu(0, k)
            sp.wait_ge(split_lo, G_END)
            for k in range(6, KD):
                load_gu(0, k)
            sp.wait_ge(group_done, G_END)
            for j in range(4):
                load_dn(0, j)
            for c in range(NB):
                sp.dma_start(b_dn[c * E:(c + 1) * E, :], b_down[0]).then_inc(b_dn_in, 16)
            for c in range(NB):
                sp.wait_ge(h2_ready, c + 1)
                sp.dma_start(h2_dram[c * P:(c + 1) * P, :], h2n[:, c, :]).then_inc(h2_stored, 16)
            for k in range(KD):
                sp.wait_ge(gu_used[k], 1)
                load_gu(1, k)
            sp.wait_ge(items_ready, 1)
            last = sp.value_load(items[0:1, LAST_AT:LAST_AT + 1], min_val=E - 1, max_val=E + MAX_EXTRA - 1)
            with sp.Fori(1, last) as i:
                e1 = sp.value_load(items[0:1, bass.ds(i + 1, 1)], min_val=0, max_val=E - 1)
                e = sp.value_load(items[0:1, bass.ds(i, 1)], min_val=0, max_val=E - 1)
                for k in range(KD):
                    sp.wait_ge(gu_used[k], i + 1)
                    load_gu(e1, k)
                for j in range(4):
                    sp.wait_ge(dn_used[j], i)
                    load_dn(e, j)
            e = sp.value_load(items[0:1, bass.ds(last, 1)], min_val=0, max_val=E - 1)
            for j in range(4):
                sp.wait_ge(dn_used[j], last)
                load_dn(e, j)
            sp.wait_ge(y_free, last + 2)
            sp.dma_start(out[0], acc_dram[0:T, :]).then_inc(out_done, 16)
            sp.wait_ge(out_done, 16)

        @block.gpsimd
        def _(pool):
            steps = [0]

            def then(ins):
                steps[0] += 1
                ins.then_inc(pool_step, 1)
                pool.wait_ge(pool_step, steps[0])

            g = nc.gpsimd
            then(g.memset(ident[:, :], 0.0))
            then(g.affine_select(out=ident[:, :], in_=ident[:, :], compare_op=ALU.not_equal, fill=1.0,
                                 base=0, pattern=[[-1, P]], channel_multiplier=1))
            g.tensor_copy(ident_b[:, :], ident[:, :]).then_inc(ident_done, 1)
            g.memset(minus_half[:, :, :], -0.5)
            g.memset(lf[:, :, :], 0.0)
            g.memset(zeros[:, :], 0.0)
            for j in range(HD // 2):
                g.memset(inv[:, j:j + 1], float(np.float32(ROPE_THETA ** (-j / (HD // 2)))))
            g.memset(upto[:, :], 1.0)
            g.memset(before_b[:, :], 1.0)
            g.memset(ones_b[:, :], 1.0)
            g.memset(c_pick[:, :], 0.0)
            then(g.memset(mask_b[:, :, :], 0.0))
            g.affine_select(out=upto[:, 0:P], in_=upto[:, 0:P], compare_op=ALU.is_ge, fill=0.0,
                            base=0, pattern=[[1, P]], channel_multiplier=-1)
            g.affine_select(out=before_b[:, :], in_=before_b[:, :], compare_op=ALU.is_gt, fill=0.0,
                            base=0, pattern=[[1, P]], channel_multiplier=-1)
            g.affine_select(out=mask_b[:, 0, :], in_=mask_b[:, 0, :], compare_op=ALU.is_gt, fill=NEG,
                            base=0, pattern=[[1, P]], channel_multiplier=-1)
            g.affine_select(out=mask_b[:, 1, :], in_=mask_b[:, 1, :], compare_op=ALU.is_ge, fill=NEG,
                            base=0, pattern=[[-1, P]], channel_multiplier=1)
            for row in range(0, P, 32):
                then(g.affine_select(out=c_pick[:, :], in_=c_pick[:, :], compare_op=ALU.not_equal, fill=1.0,
                                     base=-row, pattern=[[-1, HF]], channel_multiplier=1))
            g.tensor_copy(c_pick_r[:, :], c_pick[:, :])
            g.iota(iota_i[:, :], pattern=[[1, P]], base=0, channel_multiplier=0)
            then(g.iota(tok_i[:, :], pattern=[[P, NB]], base=0, channel_multiplier=1))
            g.tensor_copy(iota_f[:, :], iota_i[:, :])
            then(g.tensor_copy(tok_f[:, :], tok_i[:, :]))
            g.tensor_scalar(spare[:, :], tok_f[:, 0:1], float(T), None, ALU.add).then_inc(consts, 1)

            pool.wait_ge(var_ready, 1)
            g.tensor_tensor(rstd[:, 0, :], ssq[:, 0, :], minus_half[:, 0, 0:NB], ALU.pow).then_inc(rstd_ready, 1)
            pool.wait_ge(hs_var, 1)
            g.tensor_tensor(hs_r[:, :, :], hs_sum[:, :, :], minus_half[:, :, :], ALU.pow).then_inc(hs_rstd, 1)
            pool.wait_ge(group_done, G_END)
            g.memset(zero_rows[:, :], 0.0).then_inc(zero_ready, 1)
            pool.wait_ge(var_ready, 2)
            g.tensor_tensor(rstd[:, 1, :], ssq[:, 1, :], minus_half[:, 0, 0:NB], ALU.pow).then_inc(rstd_ready, 1)

            def gather():
                g.indirect_dma_start(out=xg[:, :], out_offset=None, in_=h2_dram[:, :],
                                     in_offset=bass.IndirectOffsetOnAxis(ap=idx_g[:, :], axis=0)).then_inc(xg_in, 16)

            def add_rows(n, column):
                pool.wait_ge(consts, 1)
                pool.wait_ge(y_ready, n + 1)
                g.tensor_copy(idx_s[:, :], idx_all[:, column]).then_inc(idx_s_ready, 1)
                pool.wait_ge(acc_set, 32)
                pool.wait_ge(idx_s_ready, n)
                g.indirect_dma_start(out=acc_dram[:, :],
                                     out_offset=bass.IndirectOffsetOnAxis(ap=idx_s[:, :], axis=0),
                                     in_=ysb[:, :], in_offset=None, compute_op=ALU.add).then_inc(added, 16)
                pool.wait_ge(added, n * 16)
                pool.sem_inc(y_free, 1)

            pool.sem_inc(y_free, 1)
            pool.wait_ge(h2_stored, 16 * NB)
            pool.wait_ge(idx_ready, 1)
            gather()
            pool.wait_ge(idx_ready, 2)
            pool.wait_ge(xT_ps, 1)
            gather()
            pool.wait_ge(items_ready, 1)
            n_items = pool.value_load(items[0:1, N_AT:N_AT + 1], min_val=E, max_val=E + MAX_EXTRA)
            with pool.Fori(1, n_items) as i:
                pool.wait_ge(idx_ready, i + 2)
                pool.wait_ge(xT_ps, i + 1)
                pool.sem_inc(turn, 1)
                gather()
                add_rows(i, bass.ds(i - 1, 1))
            add_rows(n_items, bass.ds(n_items - 1, 1))

        @block.scalar
        def _(act):
            sc = nc.scalar
            act.dma_start(vec_rows[0:8, :], norm1_g[0].rearrange("(r c) -> r c", c=P)).then_inc(rows_in, 16)
            act.dma_start(vec_rows[8:16, :], norm2_g[0].rearrange("(r c) -> r c", c=P)).then_inc(rows_in, 16)
            act.dma_start(vec_rows[16:32, :], b_gate[0].rearrange("(r c) -> r c", c=P)).then_inc(rows_in, 16)
            act.dma_start(bgu_rows[:, :], b_gate_up[0]).then_inc(rows_in, 16)
            act.dma_start(bf_bc[:, :], b_forget[0].partition_broadcast(P)).then_inc(small_in, 16)
            act.dma_start(sink_bc[:, :], sinks[0].partition_broadcast(P)).then_inc(small_in, 16)
            act.dma_start(brt[:, :], b_router[0].partition_broadcast(P)).then_inc(small_in, 16)
            act.dma_start(g_sw[:, 0, :], q_norm_swa[0].partition_broadcast(P)).then_inc(small_in, 16)
            act.dma_start(g_sw[:, 1, :], k_norm_swa[0].partition_broadcast(P)).then_inc(small_in, 16)
            act.dma_start(w_rt[:, :, :], w_router[0].rearrange("(k p) e -> p k e", p=P)).then_inc(small_in, 16)
            with nc.allow_non_contiguous_dma(reason="a few hundred words onto partitions"):
                act.dma_start(pos_i[:, :], positions[0].rearrange("(c p) -> p c", p=P)).then_inc(small_in, 16)
                for a, w in enumerate((q_norm_fox, k_norm_fox)):
                    for half in (0, 1):
                        act.dma_start(g_fx[half * HD:(half + 1) * HD, a:a + 1],
                                      w[0].rearrange("(d o) -> d o", o=1)).then_inc(small_in, 16)

            for c in range(NB):
                act.wait_ge(x_in[c], 16)
                sc.activation(hn_tok[:, c, :], x_tok[:, c, :], ACT.Square,
                              accum_out=ssq[:, 0, c:c + 1]).then_inc(squared, 1)

            def split_high(g):
                act.wait_ge(stage_in[g % 2], stage_waits[g])
                if g >= 2:
                    act.wait_ge(group_done, g - 1)
                sc.copy(st_h[:, g % 2], st_w[:, g % 2]).then_inc(split_hi, 1)

            split_high(0)
            act.wait_ge(wfl_in, 16)
            sc.copy(wfl_h[:, :, :], wfl[:, :, :]).then_inc(wfl_hi, 1)
            split_high(1)
            act.wait_ge(vcol_ready, 1)
            for k in range(KD):
                act.wait_ge(hT_ps, k + 1)
                sc.activation(hT_h[:, k, :], ps[:, 4 + k % 2, :], ACT.Identity,
                              scale=vcol[:, k:k + 1]).then_inc(hT_hi, 1)

            for g in range(G_GATE):
                if g >= 1:
                    split_high(g + 1)
                act.wait_ge(group_done, g + 1)
                sc.copy(tok[:, :, g * GW:(g + 1) * GW],
                        ps[:, g % 2 * 2:g % 2 * 2 + 2, :].rearrange("p b (c n) -> p (b c) n", c=2)).then_inc(group_out, 1)

            for g in range(G_GATE, G_O):
                c = g - G_GATE
                split_high(g + 1)
                if c < NB:
                    act.wait_ge(group_out, G_GATE)
                    if c >= 1:
                        act.wait_ge(sq_read, c)
                    sc.activation(sq[:, 0:SWA_H * HD], tok[:, c, 0:SWA_H * HD], ACT.Square)
                    sc.activation(sq[:, SWA_H * HD:], tok[:, c, QF:QF + FOX_H * HD], ACT.Square).then_inc(heads_sq, 1)
                if c == 1:
                    act.wait_ge(ang_ready, 1)
                    sc.activation(sin_t[:, :, :], ang[:, :, :], ACT.Sin)
                    sc.activation(cos_t[:, :, :], ang[:, :, :], ACT.Sin, scale=0.5).then_inc(sin_ready, 1)
                if c == 4:
                    act.wait_ge(fl_abs, 1)
                    sc.activation(fl_a[:, :, :], fl_a[:, :, :], ACT.Exp, scale=-1.0).then_inc(fl_exp, 1)
                    act.wait_ge(fl_exp, 1)
                    sc.activation(fl_a[:, :, :], fl_a[:, :, :], ACT.Ln, bias=1.0).then_inc(fl_ln, 1)
                act.wait_ge(group_done, g + 1)
                for d in (0, 1):
                    j = 2 * c + d
                    ins = sc.activation(gates_T[:, j, :], ps[:, g % 2 * 2 + d, :], ACT.Sigmoid,
                                        bias=vcol[:, 16 + j:17 + j])
                ins.then_inc(group_out, 1)
            split_high(G_O + 1)
            act.wait_ge(c_ps, 1)
            sc.activation(c_hi[:, :], ps[:, 7, :], ACT.Copy, scale=-1.0 / SCALE)
            for r in (0, 64):
                ins = sc.activation(c_rows[r:r + 32, :], ps[r:r + 32, 7, :], ACT.Copy, scale=-1.0 / SCALE)
            ins.then_inc(c_hi_ready, 1)

            for n in range(1, len(QKT), 2):
                s, j = QKT[n]
                act.wait_ge(qkT_ps, n + 1)
                dst, src = (qaT, kaT, qfT, kfT)[s][:, j, :], ps[:, 5, :]
                scale = 1.0 if s < 2 else g_fx[:, s - 2:s - 1]
                sc.activation(dst, src, ACT.Identity, scale=scale).then_inc(qkT_out[1], 1)

            for n in range(NU):
                act.wait_ge(shift, n + 1)
                if n >= 3:
                    act.wait_ge(pT_ps, n - 2)
                w = width(n)
                sc.activation(p_sb[:, n % 3, 0:w], ps[:, n % 4, 0:w], ACT.Exp, bias=nb[:, n:n + 1],
                              scale=SCALE, accum_out=den[:, n:n + 1]).then_inc(probs, 1)
                if n % 16 == 9:
                    act.wait_ge(snk_in, n // 16 + 1)
                    sc.activation(snk[:, :], snk[:, :], ACT.Exp).then_inc(snk_exp, 1)
            for k in range(KD):
                act.wait_ge(oT_ps, k + 1)
                sc.copy(oT_h[:, k, :], ps[:, k % 4, :]).then_inc(oT_hi, 1)
            for g in range(G_O, G_OUT):
                if g > G_O:
                    split_high(g + 1)
                for j in (2 * (g - G_O), 2 * (g - G_O) + 1):
                    act.wait_ge(m_sum, j + 1)
                    sc.copy(mT_h[:, j, :], merge_s[:, j % 2, :]).then_inc(m_hi, 1)
            for g in range(G_OUT + 1, G_END):
                split_high(g)
            for c in range(NB):
                act.wait_ge(x1_ready, N_OUT)
                sc.activation(h2n[:, c, :], x_tok[:, c, :], ACT.Square,
                              accum_out=ssq[:, 1, c:c + 1]).then_inc(squared, 1)
            for k in range(1, KD, 2):
                act.wait_ge(h2T_ps, k + 1)
                sc.activation(h2T[:, k, :], ps[:, 5, :], ACT.Identity,
                              scale=vcol[:, 8 + k:9 + k]).then_inc(h2T_out[1], 1)
            act.wait_ge(r_shifted, 1)
            sc.activation(r_ex[:, :, :], r_ex[:, :, :], ACT.Exp).then_inc(r_exp, 1)
            act.wait_ge(gateT_ps, 1)
            sc.copy(gateT[:, :], ps[:, 5, 0:P]).then_inc(gateT_ready, 1)

            def sigmoid(i, first=False):
                act.wait_ge(g_ready, i + 1)
                if not first:
                    act.wait_ge(gs_ready, i)
                sc.activation(act_s[:, :, :], act_g[:, :, :], ACT.Sigmoid, scale=ALPHA).then_inc(sig_ready, 1)

            def down_high(n):
                for j in range(4):
                    act.wait_ge(consts, 1)
                    act.wait_ge(dn_in[j], n * 16)
                    sc.copy(wdn_h[:, j], wdn[:, j]).then_inc(dn_hi[j], 1)

            def act_high(i):
                act.wait_ge(a_whole, i + 1)
                sc.copy(aT_h[:, :, :], aT[:, :, :]).then_inc(a_hi, 1)

            def weigh(n, column):
                act.wait_ge(consts, 1)
                act.wait_ge(dn_used[3], n)
                act.wait_ge(y_free, n)
                sc.activation(ysb[:, :].rearrange("p (b n) -> p b n", b=2), ps[0:SLOTS, 4:6, :], ACT.Identity,
                              scale=gate_all[:, column]).then_inc(y_ready, 1)

            sigmoid(0, first=True)
            act_high(0)
            act.wait_ge(bdn_out, 8)
            act.dma_start(acc_dram[0:T, :].rearrange("(c p) d -> p c d", p=P), x_tok[:, :, :]).then_inc(acc_set, 16)
            act.wait_ge(zero_ready, 1)
            act.dma_start(acc_dram[T:T + SLOTS, :], zero_rows[:, :]).then_inc(acc_set, 16)
            act.wait_ge(items_ready, 1)
            n_items = act.value_load(items[0:1, N_AT:N_AT + 1], min_val=E, max_val=E + MAX_EXTRA)
            with act.Fori(1, n_items) as i:
                down_high(i)
                sigmoid(i)
                act_high(i)
                weigh(i, bass.ds(i - 1, 1))
            down_high(n_items)
            weigh(n_items, bass.ds(n_items - 1, 1))

        @block.vector
        def _(dve):
            v = nc.vector
            steps = [0]

            def then(ins):
                steps[0] += 1
                ins.then_inc(dve_step, 1)
                dve.wait_ge(dve_step, steps[0])

            def split_low(g):
                dve.wait_ge(split_hi, g + 1)
                v.tensor_tensor(st_l[:, g % 2], st_w[:, g % 2], st_h[:, g % 2].bitcast(F32),
                                ALU.subtract).then_inc(split_lo, 1)

            dve.wait_ge(squared, NB)
            v.tensor_scalar(ssq[:, 0, :], ssq[:, 0, :], 1.0 / D, EPS, ALU.mult, ALU.add).then_inc(var_ready, 1)
            dve.wait_ge(rows_ps, 1)
            v.tensor_copy(vcol[:, :], ps[:, 6, 0:32]).then_inc(vcol_ready, 1)
            dve.wait_ge(rstd_ready, 1)
            for c in range(NB):
                v.tensor_scalar(hn_tok[:, c, :], x_tok[:, c, :], rstd[:, 0, c:c + 1], None, ALU.mult).then_inc(hn_ready, 1)
            split_low(0)
            dve.wait_ge(vcol_ready, 1)
            for k in range(KD):
                dve.wait_ge(hT_hi, k + 1)
                v.scalar_tensor_tensor(out=hT_l[:, k, :], in0=ps[:, 4 + k % 2, :], scalar=vcol[:, k:k + 1],
                                       in1=hT_h[:, k, :].bitcast(F32), op0=ALU.mult,
                                       op1=ALU.subtract).then_inc(hT_ready, 1)
            split_low(1)
            dve.wait_ge(wfl_hi, 1)
            v.tensor_tensor(wfl_l[:, :, :], wfl[:, :, :], wfl_h[:, :, :].bitcast(F32), ALU.subtract).then_inc(wfl_ready, 1)
            dve.wait_ge(rows_ps, 2)
            v.tensor_copy(bgu[:, :, :].rearrange("p e j -> p j e"),
                          ps[:, 7, :].rearrange("p (j e) -> p j e", e=E)).then_inc(bgu_ready, 1)
            dve.wait_ge(consts, 1)
            dve.wait_ge(small_in, 16 * 11)
            then(v.tensor_copy(pos_f[:, :], pos_i[:, :]))
            then(v.tensor_tensor(ang[:, :, :], bc(pos_f[:, :], 2, HD // 2), bc(inv[:, :], 1, NB), ALU.mult))
            then(v.tensor_scalar(ang_k[:, :, :], ang[:, :, :], float(1.0 / TWO_PI), MAGIC, ALU.mult, ALU.add))
            then(v.tensor_scalar(ang_k[:, :, :], ang_k[:, :, :], -MAGIC, None, ALU.add))
            for part in (C1, C2, C3):
                then(v.scalar_tensor_tensor(out=ang[:, :, :], in0=ang_k[:, :, :], scalar=-part, in1=ang[:, :, :],
                                            op0=ALU.mult, op1=ALU.add))
            v.tensor_scalar(ang[:, :, :], ang[:, :, :], 3.1415925, -3.1415925, ALU.min, ALU.max).then_inc(ang_ready, 1)
            v.tensor_scalar(sink8[:, :], sink_bc[:, :], 1.0 / SCALE, None, ALU.mult)
            for g in range(2, G_GATE + 1):
                split_low(g)

            dve.wait_ge(fl_ps, 1)
            then(v.tensor_tensor(fl[:, :, :], ps[:, 6, 0:NB * HF].rearrange("p (c h) -> p c h", c=NB),
                                 bc(bf_bc[:, :], 1, NB), ALU.add))
            v.scalar_tensor_tensor(out=fl_a[:, :, :], in0=fl[:, :, :], scalar=-1.0, in1=fl[:, :, :],
                                   op0=ALU.mult, op1=ALU.max).then_inc(fl_abs, 1)

            heads_a = [tok[:, c, 0:SWA_H * HD].rearrange("p (h d) -> p h d", d=HD) for c in range(NB)]
            heads_f = [tok[:, c, QF:QF + FOX_H * HD].rearrange("p (h d) -> p h d", d=HD) for c in range(NB)]
            for g in range(G_GATE, G_O):
                c = g - G_GATE
                split_low(g + 1)
                if c < NB:
                    dve.wait_ge(heads_sq, c + 1)
                    v.tensor_reduce(hs_sum[:, c, :], sq[:, :].rearrange("p (h d) -> p h d", d=HD),
                                    AX.X, ALU.add).then_inc(sq_read, 1)
                if c == NB - 1:
                    dve.wait_ge(sq_read, NB)
                    v.tensor_scalar(hs_sum[:, :, :], hs_sum[:, :, :], 1.0 / HD, EPS, ALU.mult, ALU.add).then_inc(hs_var, 1)
                    dve.wait_ge(sin_ready, 1)
                    then(v.tensor_tensor(cos_t[:, :, :], cos_t[:, :, :], cos_t[:, :, :], ALU.mult))
                    then(v.tensor_scalar(cos_t[:, :, :], cos_t[:, :, :], -2.0, 1.0, ALU.mult, ALU.add))
                    H2 = HD // 2
                    for a in (0, 1):
                        g1, g2 = bc(g_sw[:, a, 0:H2], 1, NB), bc(g_sw[:, a, H2:HD], 1, NB)
                        v.tensor_tensor(rope_c[:, a, :, 0:H2], cos_t[:, :, :], g1, ALU.mult)
                        v.tensor_tensor(rope_c[:, a, :, H2:HD], cos_t[:, :, :], g2, ALU.mult)
                        v.tensor_tensor(rope_s[:, a, :, H2:HD], sin_t[:, :, :], g1, ALU.mult)
                        then(v.scalar_tensor_tensor(out=rope_s[:, a, :, 0:H2], in0=sin_t[:, :, :], scalar=-1.0,
                                                    in1=g2, op0=ALU.mult, op1=ALU.mult))
                    dve.wait_ge(hs_rstd, 1)
                if c >= NB:
                    c -= NB
                    v.tensor_tensor(heads_f[c], heads_f[c], bc(hs_r[:, c, SWA_H:HN], 2, HD), ALU.mult)
                    then(v.tensor_tensor(heads_a[c], heads_a[c], bc(hs_r[:, c, 0:SWA_H], 2, HD), ALU.mult))
                    for a, h0, h1 in ((0, 0, HQ), (1, HQ, SWA_H)):
                        n = h1 - h0
                        v.tensor_tensor(rot[:, 0, h0:h1, :], heads_a[c][:, h0:h1, :], bc(rope_c[:, a, c, :], 1, n), ALU.mult)
                        v.tensor_tensor(rot[:, 1, h0:h1, 0:H2], heads_a[c][:, h0:h1, H2:HD],
                                        bc(rope_s[:, a, c, 0:H2], 1, n), ALU.mult)
                        then(v.tensor_tensor(rot[:, 1, h0:h1, H2:HD], heads_a[c][:, h0:h1, 0:H2],
                                             bc(rope_s[:, a, c, H2:HD], 1, n), ALU.mult))
                    v.tensor_tensor(heads_a[c][:, 0:HQ, :], rot[:, 0, 0:HQ, :], rot[:, 1, 0:HQ, :], ALU.add)
                    for half in (0, 1):
                        ins = v.tensor_tensor(k_dup[:, c, :, half, :], rot[:, 0, HQ:SWA_H, :], rot[:, 1, HQ:SWA_H, :],
                                              ALU.add)
                    ins.then_inc(qk_ready, 1)
                if g == G_GATE + 5:
                    dve.wait_ge(fl_ln, 1)
                    for at in range(0, P, 32):
                        ins = v.scalar_tensor_tensor(out=lf[:, :, at:at + HF], in0=fl[:, :, :], scalar=0.0,
                                                     in1=fl_a[:, :, :], op0=ALU.min, op1=ALU.subtract)
                    ins.then_inc(lf_ready, 1)
            split_low(G_O + 1)
            dve.wait_ge(c_hi_ready, 1)
            for r in (32, 96):
                ins = v.scalar_tensor_tensor(out=c_rows[r:r + 32, :], in0=ps[r:r + 32, 7, :], scalar=-1.0 / SCALE,
                                             in1=c_hi[r:r + 32, :].bitcast(F32), op0=ALU.mult, op1=ALU.subtract)
            ins.then_inc(c_ready, 1)
            for n in range(0, len(QKT), 2):
                s, j = QKT[n]
                dve.wait_ge(qkT_ps, n + 1)
                dst, src = (qaT, kaT, qfT, kfT)[s][:, j, :], ps[:, 4, :]
                scale = 1.0 if s < 2 else g_fx[:, s - 2:s - 1]
                v.tensor_scalar(dst, src, scale, None, ALU.mult).then_inc(qkT_out[0], 1)

            def finish_block(u):
                c, b = u // 2, u % 2
                dve.wait_ge(probs, 8 * u + 8)
                sums = den[:, 8 * u:8 * u + 8]
                if b == 0:
                    dve.wait_ge(snk_exp, c + 1)
                    then(v.tensor_tensor(sums, sums, snk[:, :], ALU.add))
                then(v.reciprocal(rden[:, 8 * u:8 * u + 8], sums))
                dve.wait_ge(pv_done, 8 * u + 8)
                v.tensor_tensor(o_tok[:, c, b * QW:(b + 1) * QW].rearrange("p (h d) -> p h d", d=HD),
                                ps[:, 6 + b, :].rearrange("p (h d) -> p h d", d=HD),
                                bc(rden[:, 8 * u:8 * u + 8], 2, HD), ALU.mult).then_inc(o_out, 1)

            for n in range(NU + 5):
                if n < NU:
                    c, b, h = units[n]
                    dve.wait_ge(scores, n + 1)
                    v.reduce_max(mx[:, n:n + 1], ps[:, n % 4, 0:width(n)], AX.X).then_inc(maxed, 1)
                if 2 <= n < NU + 2:
                    m = n - 2
                    dve.wait_ge(pT_ps, m + 1)
                    if m >= 2:
                        dve.wait_ge(pv_done, m - 1)
                    v.tensor_copy(pT_sb[:, m % 2, 0:width(m)], ps[:, 4 + m % 2, 0:width(m)]).then_inc(pT_ready, 1)
                if n < NU:
                    dve.wait_ge(maxed, n + 1)
                    if b == 0:
                        v.tensor_scalar(nb[:, n:n + 1], mx[:, n:n + 1], sink8[:, h:h + 1], -SCALE,
                                        ALU.max, ALU.mult).then_inc(shift, 1)
                    else:
                        v.tensor_scalar(nb[:, n:n + 1], mx[:, n:n + 1], -SCALE, None, ALU.mult).then_inc(shift, 1)
                    if b == 0 and h == 7:
                        dve.wait_ge(shift, n + 1)
                        v.tensor_tensor(snk[:, :], sink_bc[:, :], nb[:, n - 7:n + 1], ALU.add).then_inc(snk_in, 1)
                if n >= 12 and (n - 12) % 8 == 0:
                    finish_block((n - 12) // 8)
            for k in range(KD):
                dve.wait_ge(oT_hi, k + 1)
                v.tensor_tensor(oT_l[:, k, :], ps[:, k % 4, :], oT_h[:, k, :].bitcast(F32), ALU.subtract).then_inc(oT_ready, 1)

            def merge_low(j):
                dve.wait_ge(m_hi, j + 1)
                v.tensor_tensor(mT_l[:, j, :], merge_s[:, j % 2, :], mT_h[:, j, :].bitcast(F32),
                                ALU.subtract).then_inc(m_ready, 1)

            for g in range(G_O, G_OUT):
                if g > G_O:
                    split_low(g + 1)
                dve.wait_ge(group_done, g + 1)
                for d in (0, 1):
                    j, bank = 2 * (g - G_O) + d, (g - G_O) % 2 * 4 + 2 * d
                    if j >= 1:
                        dve.wait_ge(m_sum, j)
                    v.tensor_tensor(merge_t[:, 0, :], ps[:, bank, :], gates_T[:, j, :], ALU.mult)
                    v.tensor_tensor(merge_t[:, 1, :], ps[:, bank + 1, :], gates_T[:, KD + j, :], ALU.mult).then_inc(m_part, 1)
                    if j >= 1:
                        merge_low(j - 1)
                    dve.wait_ge(m_part, j + 1)
                    if j >= 2:
                        dve.wait_ge(m_ready, j - 1)
                    v.tensor_tensor(merge_s[:, j % 2, :], merge_t[:, 0, :], merge_t[:, 1, :], ALU.add).then_inc(m_sum, 1)
            merge_low(KD - 1)
            for g in range(G_OUT, G_END):
                if G_OUT < g:
                    split_low(g)
                if g > G_OUT:
                    add_group = g - 1
                else:
                    continue
                dve.wait_ge(group_done, add_group + 1)
                n0, b0 = (add_group - G_OUT) * GW, (add_group - G_OUT) % 2 * 2
                v.tensor_tensor(x_tok[:, :, n0:n0 + GW], x_tok[:, :, n0:n0 + GW],
                                ps[:, b0:b0 + 2, :].rearrange("p b (c n) -> p (b c) n", c=2), ALU.add).then_inc(x1_ready, 1)
            add_group = G_END - 1
            dve.wait_ge(group_done, add_group + 1)
            n0, b0 = (add_group - G_OUT) * GW, (add_group - G_OUT) % 2 * 2
            v.tensor_tensor(x_tok[:, :, n0:n0 + GW], x_tok[:, :, n0:n0 + GW],
                            ps[:, b0:b0 + 2, :].rearrange("p b (c n) -> p (b c) n", c=2), ALU.add).then_inc(x1_ready, 1)
            dve.wait_ge(squared, 2 * NB)
            v.tensor_scalar(ssq[:, 1, :], ssq[:, 1, :], 1.0 / D, EPS, ALU.mult, ALU.add).then_inc(var_ready, 1)
            dve.wait_ge(rstd_ready, 2)
            for c in range(NB):
                v.tensor_scalar(h2n[:, c, :], x_tok[:, c, :], rstd[:, 1, c:c + 1], None, ALU.mult).then_inc(h2_ready, 1)
            for k in range(0, KD, 2):
                dve.wait_ge(h2T_ps, k + 1)
                v.tensor_scalar(h2T[:, k, :], ps[:, 4, :], vcol[:, 8 + k:9 + k], None, ALU.mult).then_inc(h2T_out[0], 1)

            dve.wait_ge(logits_ps, 1)
            then(v.tensor_tensor(lg[:, :, :], ps[:, 6, 0:NB * E].rearrange("p (c e) -> p c e", c=NB), bc(brt[:, :], 1, NB), ALU.add))
            for c in range(NB):
                ins = v.max(top8[:, c, :], lg[:, c, :])
            then(ins)
            least = bc(top8[:, :, TOP_K - 1], 2, E)
            v.tensor_tensor(r_ex[:, :, :], lg[:, :, :], bc(top8[:, :, 0], 2, E), ALU.subtract).then_inc(r_shifted, 1)
            v.tensor_tensor(r_eq[:, :, :], lg[:, :, :], least, ALU.is_equal)
            then(v.tensor_tensor(r_gt[:, :, :], lg[:, :, :], least, ALU.is_gt))
            v.tensor_reduce(need[:, :], r_gt[:, :, :], AX.X, ALU.add)
            for c in range(NB):
                ins = v.tensor_tensor_scan(r_in[:, c, :], r_eq[:, c, :], zeros[:, 0:E], 0.0, ALU.add, ALU.add)
            then(ins)
            then(v.tensor_scalar(need[:, :], need[:, :], -1.0, float(TOP_K), ALU.mult, ALU.add))
            then(v.tensor_tensor(r_in[:, :, :], r_in[:, :, :], bc(need[:, :], 2, E), ALU.is_le))
            then(v.tensor_tensor(r_eq[:, :, :], r_eq[:, :, :], r_in[:, :, :], ALU.mult))
            then(v.tensor_tensor(r_eq[:, :, :], r_eq[:, :, :], r_gt[:, :, :], ALU.add))
            v.tensor_copy(sel_b[:, :, :], r_eq[:, :, :]).then_inc(picked, 1)
            dve.wait_ge(r_exp, 1)
            then(v.tensor_tensor(r_ex[:, :, :], r_ex[:, :, :], r_eq[:, :, :], ALU.mult))
            then(v.tensor_reduce(zsum[:, :], r_ex[:, :, :], AX.X, ALU.add))
            then(v.reciprocal(zsum[:, :], zsum[:, :]))
            v.tensor_tensor(r_gt[:, :, :], r_ex[:, :, :], bc(zsum[:, :], 2, E), ALU.mult).then_inc(gates_ready, 1)
            for c in range(NB):
                v.tensor_scalar(row_tab[:, c, :, 0], zeros[:, :], tok_f[:, c:c + 1], -BIG, ALU.add, ALU.add)
            dve.wait_ge(gates_ready, 1)
            v.tensor_copy(row_tab[:, :, 0:E, 1], r_gt[:, :, :])
            v.memset(row_tab[:, :, ITEMS - 1:ITEMS, 1], 0.0)
            v.memset(slot_tab[:, :, ITEMS - 1:ITEMS], -1.0)
            dve.wait_ge(place_ps, 1)
            v.tensor_copy(cnt[:, :], ps[:, 4, 0:E])
            then(v.scalar_tensor_tensor(out=r_in[:, :, :], in0=ps[:, 7, 0:NB * E].rearrange("p (c e) -> p c e", c=NB),
                                        scalar=1.0, in1=r_eq[:, :, :], op0=ALU.add, op1=ALU.mult))
            then(v.tensor_scalar(slot_tab[:, :, 0:E], r_in[:, :, :], -1.0, None, ALU.add))

            def pick(i, first=False):
                if not first:
                    dve.wait_ge(list_ps, i)
                for c in range(NB):
                    ins = v.tensor_scalar(sel[:, c, :], iota_f[:, 0:SLOTS],
                                          slot_tab[:, c, i:i + 1] if isinstance(i, int) else slot_tab[:, c, bass.ds(i, 1)],
                                          None, ALU.is_equal)
                ins.then_inc(sel_ready, 1)

            def index(i, first=False):
                col = slice(i, i + 1) if isinstance(i, int) else bass.ds(i, 1)
                dve.wait_ge(list_ps, i + 1)
                if not first:
                    dve.wait_ge(xg_in, i * 16)
                v.tensor_scalar(idx_g[:, :], list_v[:, 0:1], BIG, float(T - 1), ALU.add, ALU.min)
                v.tensor_scalar(idx_all[:, col], list_v[:, 0:1], BIG, spare[0:SLOTS, :], ALU.add, ALU.min)
                v.tensor_copy(gate_all[:, col], list_v[:, 1:2]).then_inc(idx_ready, 1)

            def move_rows(i, first=False):
                dve.wait_ge(xT_ps, i + 1)
                if not first:
                    dve.wait_ge(gu_used[KD - 1], i)
                v.tensor_tensor(xT[:, :, :], xT_ps_v, bc(vcol[:, 8:8 + KD], 2, SLOTS), ALU.mult).then_inc(xT_ready, 1)

            def activate(i, e, first=False):
                at = bgu[:, e, :] if isinstance(e, int) else bgu[:, bass.ds(e, 1), :].rearrange("p a j -> p (a j)")
                if not first:
                    dve.wait_ge(a_ready, i)
                dve.wait_ge(gu_used[KD - 1], i + 1)
                v.tensor_tensor(act_g[:, :, :], gu_v[:, 0:KD], bc(at[:, 0:KD], 2, SLOTS), ALU.add).then_inc(g_biased, 1)
                v.tensor_tensor(act_u[:, :, :], gu_v[:, KD:2 * KD], bc(at[:, KD:2 * KD], 2, SLOTS), ALU.add).then_inc(gu_out, 1)
                dve.wait_ge(g_biased, i + 1)
                v.tensor_scalar(act_g[:, :, :], act_g[:, :, :], LIMIT, None, ALU.min).then_inc(g_ready, 1)
                dve.wait_ge(gu_out, i + 1)
                v.tensor_scalar(act_u[:, :, :], act_u[:, :, :], LIMIT, -LIMIT, ALU.min, ALU.max).then_inc(u_ready, 1)
                dve.wait_ge(sig_ready, i + 1)
                v.tensor_tensor(act_g[:, :, :], act_g[:, :, :], act_s[:, :, :], ALU.mult).then_inc(gs_ready, 1)
                dve.wait_ge(gs_ready, i + 1)
                dve.wait_ge(u_ready, i + 1)
                if not first:
                    dve.wait_ge(dn_used[3], i)
                v.scalar_tensor_tensor(out=aT[:, :, :], in0=act_u[:, :, :], scalar=1.0, in1=act_g[:, :, :],
                                       op0=ALU.add, op1=ALU.mult).then_inc(a_whole, 1)
                dve.wait_ge(a_hi, i + 1)
                v.tensor_tensor(aT_l[:, :, :], aT[:, :, :], aT_h[:, :, :].bitcast(F32),
                                ALU.subtract).then_inc(a_ready, 1)

            def down_low(n):
                for j in range(4):
                    dve.wait_ge(dn_hi[j], n)
                    v.tensor_tensor(wdn_l[:, j], wdn[:, j], wdn_h[:, j].bitcast(F32),
                                    ALU.subtract).then_inc(dn_lo[j], 1)

            pick(0, first=True)
            index(0, first=True)
            then(v.tensor_scalar(ext[:, :], cnt[:, :], float(SLOTS), None, ALU.is_gt))
            for j in range(2, LEVELS + 1):
                then(v.scalar_tensor_tensor(out=ext[:, :], in0=cnt[:, :], scalar=float(SLOTS * j), in1=ext[:, :],
                                            op0=ALU.is_gt, op1=ALU.add))
            then(v.tensor_tensor_scan(ext_in[:, :], ext[:, :], zeros[:, 0:E], 0.0, ALU.add, ALU.add))
            v.tensor_tensor(ext_ex[:, :], ext_in[:, :], ext[:, :], ALU.subtract)
            number = iota_f[:, 0:MAX_EXTRA]
            then(v.tensor_tensor(onehot_t[:, :, :], bc(ext_in[:, :], 1, MAX_EXTRA), bc(number, 2, E), ALU.is_le))
            then(v.tensor_reduce(item_e[:, :], onehot_t[:, :, :], AX.X, ALU.add))
            then(v.memset(items_f[:, :], 0.0))
            v.tensor_tensor(onehot[:, :, :], bc(iota_f[:, 0:E], 1, MAX_EXTRA), bc(item_e[:, :], 2, E), ALU.is_equal)
            then(v.tensor_scalar(item_b[:, :], item_e[:, :], float(E - 1), None, ALU.min))
            v.tensor_copy(items_f[:, 0:E], iota_f[0:1, 0:E])
            v.tensor_copy(items_f[:, E:E + MAX_EXTRA], item_b[0:1, :])
            v.tensor_scalar(items_f[:, LAST_AT:LAST_AT + 1], ext_in[0:1, E - 1:E], float(E - 1), None, ALU.add)
            then(v.tensor_scalar(items_f[:, N_AT:N_AT + 1], ext_in[0:1, E - 1:E], float(E), None, ALU.add))
            v.tensor_copy(items[:, :], items_f[:, :]).then_inc(items_ready, 1)
            move_rows(0, first=True)
            pick(1)
            index(1)
            then(v.tensor_tensor(onehot_t[:, :, :], onehot[:, :, :], bc(ext_ex[:, :], 1, MAX_EXTRA), ALU.mult))
            then(v.tensor_reduce(item_b[:, :], onehot_t[:, :, :], AX.X, ALU.add))
            then(v.tensor_tensor(item_b[:, :], number, item_b[:, :], ALU.subtract))
            then(v.tensor_scalar(item_b[:, :], item_b[:, :], float(SLOTS), float(SLOTS), ALU.mult, ALU.add))
            for c in range(NB):
                then(v.tensor_tensor(onehot_t[:, :, :], onehot[:, :, :], bc(r_gt[:, c, :], 1, MAX_EXTRA), ALU.mult))
                then(v.tensor_reduce(row_tab[:, c, E:E + MAX_EXTRA, 1], onehot_t[:, :, :], AX.X, ALU.add))
                then(v.tensor_tensor(onehot_t[:, :, :], onehot[:, :, :], bc(slot_tab[:, c, 0:E], 1, MAX_EXTRA), ALU.mult))
                then(v.tensor_reduce(slot_tab[:, c, E:E + MAX_EXTRA], onehot_t[:, :, :], AX.X, ALU.add))
                then(v.tensor_tensor(slot_tab[:, c, E:E + MAX_EXTRA], slot_tab[:, c, E:E + MAX_EXTRA], item_b[:, :],
                                     ALU.subtract))
            move_rows(1)
            activate(0, 0, first=True)
            for m in range(8):
                c, n0 = m // 2, m % 2 * 512
                dve.wait_ge(bdn_ps, m + 1)
                ins = v.tensor_tensor(x_tok[:, c, n0:n0 + 512], x_tok[:, c, n0:n0 + 512], ps[:, 4 + m % 2, :],
                                      ALU.add).then_inc(bdn_out, 1)
            dve.wait_ge(bdn_out, 8)
            v.memset(need[:, 0:1], 0.0).then_inc(y_ready, 1)
            n_items = dve.value_load(items[0:1, N_AT:N_AT + 1], min_val=E, max_val=E + MAX_EXTRA)
            with dve.Fori(1, n_items) as i:
                e = dve.value_load(items[0:1, bass.ds(i, 1)], min_val=0, max_val=E - 1)
                pick(i + 1)
                index(i + 1)
                down_low(i)
                move_rows(i + 1)
                activate(i, e)
            down_low(n_items)

        @block.tensor
        def _(pe):
            pe.wait_ge(ident_done, 1)
            pe.wait_ge(rows_in, 64)
            pe.transpose(ps[:, 6, 0:32], vec_rows[:, :], ident[0:32, 0:32]).then_inc(rows_ps, 1)
            for j in range(2 * KD):
                ins = pe.transpose(ps[:, 7, j * E:(j + 1) * E], bgu_rows[:, j * P:(j + 1) * P], ident[0:E, 0:E])
            ins.then_inc(rows_ps, 1)

            for k in range(KD):
                if k == 0:
                    pe.wait_ge(hn_ready, NB)
                if k >= 2:
                    pe.wait_ge(hT_ready, k - 1)
                for c in range(NB):
                    ins = pe.transpose(ps[:, 4 + k % 2, c * P:(c + 1) * P], hn_tok[:, c, k * P:(k + 1) * P], ident[:, :])
                ins.then_inc(hT_ps, 1)

            def rows_times_group(dst, xh, xl, wh, wl):
                n = xh.shape[1]
                for k in range(n):
                    pe.matmul(dst, xh[:, k], wh[:, k], start=(k == 0), stop=False)
                    pe.matmul(dst, xh[:, k], wl[:, k], start=False, stop=False)
                    ins = pe.matmul(dst, xl[:, k], wh[:, k], start=False, stop=(k == n - 1))
                return ins

            def group_times_rows(dst, wh, wl, xh, xl):
                n = wh.shape[1]
                for k in range(n):
                    pe.matmul(dst, wh[:, k], xh[:, k], start=(k == 0), stop=False)
                    pe.matmul(dst, wh[:, k], xl[:, k], start=False, stop=False)
                    ins = pe.matmul(dst, wl[:, k], xh[:, k], start=False, stop=(k == n - 1))
                return ins

            def token_group(bank, buffer, xh, xl):
                for c in range(NB):
                    dst = ps[:, bank + c // 2, c % 2 * GW:(c % 2 + 1) * GW]
                    s = slice(c * P, (c + 1) * P)
                    ins = rows_times_group(dst, xh[:, :, s], xl[:, :, s], st_h[:, buffer], st_l[:, buffer])
                ins.then_inc(group_done, 1)

            pe.wait_ge(hT_ready, KD)
            for g in (0, 1):
                pe.wait_ge(split_lo, g + 1)
                token_group(2 * g, g, hT_h, hT_l)
            with pe.Fori(0, G_GATE // 2 - 1) as pair:
                for b in (0, 1):
                    pe.wait_ge(split_lo, pair * 2 + (b + 3))
                    pe.wait_ge(group_out, pair * 2 + (b + 1))
                    token_group(2 * b, b, hT_h, hT_l)
            pe.wait_ge(split_lo, G_GATE)
            pe.wait_ge(group_out, G_GATE - 2)
            token_group(0, 0, hT_h, hT_l)
            pe.wait_ge(wfl_ready, 1)
            pe.wait_ge(vcol_ready, 1)
            for c in range(NB):
                s = slice(c * P, (c + 1) * P)
                ins = rows_times_group(ps[:, 6, c * HF:(c + 1) * HF], hT_h[:, :, s], hT_l[:, :, s], wfl_h, wfl_l)
            ins.then_inc(fl_ps, 1)

            def gate_group(b):
                for d in (0, 1):
                    s = slice(d * P, (d + 1) * P)
                    ins = group_times_rows(ps[:, 2 * b + d, :], st_h[:, b, :, s], st_l[:, b, :, s], hT_h, hT_l)
                ins.then_inc(group_done, 1)

            with pe.Fori(0, N_GATE // 2) as pair:
                for b in (0, 1):
                    pe.wait_ge(split_lo, pair * 2 + (G_GATE + b + 1))
                    pe.wait_ge(group_out, pair * 2 + (G_GATE + b - 1))
                    gate_group((G_GATE + b) % 2)

            pe.wait_ge(lf_ready, 1)
            pe.wait_ge(bgu_ready, 1)
            for c in range(NB):
                ins = pe.matmul(ps[:, 7, c * P:T], lf[:, c, :], upto[:, 0:T - c * P], start=(c == 0), stop=(c == NB - 1))
            ins.then_inc(c_ps, 1)

            pe.wait_ge(qk_ready, NB)
            for n, (s, j) in enumerate(QKT):
                if n >= 2:
                    pe.wait_ge(qkT_out[n % 2], n // 2)
                for c in range(NB):
                    c0 = (0, None, QF, KF)[s]
                    src = k_dup[:, c, j].rearrange("p a d -> p (a d)") if s == 1 else tok[:, c, c0 + j * P:c0 + (j + 1) * P]
                    ins = pe.transpose(ps[:, 4 + n % 2, c * P:(c + 1) * P], src, ident[:, :])
                ins.then_inc(qkT_ps, 1)

            def unit_scores(n):
                c, fox, h = units[n]
                w, bank = width(n), n % 4
                if n >= 4:
                    pe.wait_ge(probs, n - 3)
                rows = slice(h % 2 * HD, (h % 2 + 1) * HD)
                q = (qfT if fox else qaT)[rows, h // 2, c * P:(c + 1) * P]
                k0 = (c + 1) * P - w
                kv = kfT[rows, h // 2, k0:k0 + w] if fox else kaT[rows, h // (HQ // KV), k0:k0 + w]
                pe.matmul(ps[:, bank, 0:w], q, kv, start=True, stop=False)
                if fox:
                    pe.matmul(ps[:, bank, 0:w], c_pick_r[rows, h:h + 1].broadcast_to([HD, P]), c_rows[rows, 0:w],
                              start=False, stop=False)
                    ins = pe.matmul(ps[:, bank, w - P:w], ident_b[:, :], mask_b[:, 1, :], start=False, stop=True)
                else:
                    m = mask_b[:, :, :].rearrange("p a k -> p (a k)")[:, 2 * P - w:2 * P]
                    ins = pe.matmul(ps[:, bank, 0:w], ident_b[:, :], m, start=False, stop=True)
                ins.then_inc(scores, 1)

            def unit_transposes(n):
                pe.wait_ge(probs, n + 1)
                if n >= 2:
                    pe.wait_ge(pT_ready, n - 1)
                for kb in range(width(n) // P):
                    ins = pe.transpose(ps[:, 4 + n % 2, kb * P:(kb + 1) * P], p_sb[:, n % 3, kb * P:(kb + 1) * P], ident[:, :])
                ins.then_inc(pT_ps, 1)

            def unit_values(n):
                c, fox, h = units[n]
                u, nk = n // 8, width(n) // P
                pe.wait_ge(pT_ready, n + 1)
                if n % 8 == 0 and u >= 2:
                    pe.wait_ge(o_out, u - 1)
                v0 = VF + h * HD if fox else VA + h // (HQ // KV) * HD
                for kb in range(nk):
                    ins = pe.matmul(ps[:, 6 + fox, h * HD:(h + 1) * HD], pT_sb[:, n % 2, kb * P:(kb + 1) * P],
                                    tok[:, c + 1 - nk + kb, v0:v0 + HD], start=(kb == 0), stop=(kb == nk - 1))
                ins.then_inc(pv_done, 1)

            pe.wait_ge(c_ready, 1)
            pe.wait_ge(group_out, G_O)
            pe.wait_ge(qkT_out[0], (len(QKT) + 1) // 2)
            pe.wait_ge(qkT_out[1], len(QKT) // 2)
            for n in range(NU + 3):
                if n < NU:
                    unit_scores(n)
                if 2 <= n < NU + 2:
                    unit_transposes(n - 2)
                if n >= 3:
                    unit_values(n - 3)

            pe.wait_ge(o_out, 2 * NB)
            for k in range(KD):
                if k >= 4:
                    pe.wait_ge(oT_ready, k - 3)
                for c in range(NB):
                    ins = pe.transpose(ps[:, k % 4, c * P:(c + 1) * P], o_tok[:, c, k * P:(k + 1) * P], ident[:, :])
                ins.then_inc(oT_ps, 1)
            pe.wait_ge(oT_ready, KD)
            for g in range(G_O, G_OUT):
                pe.wait_ge(split_lo, g + 1)
                if g >= G_O + 2:
                    pe.wait_ge(m_sum, 2 * (g - G_O - 1))
                for d in (0, 1):
                    s = slice(d * P, (d + 1) * P)
                    for branch in (0, 1):
                        kk = slice(4 * branch, 4 * branch + 4)
                        ins = group_times_rows(ps[:, (g - G_O) % 2 * 4 + 2 * d + branch, :], st_h[:, g % 2, kk, s],
                                               st_l[:, g % 2, kk, s], oT_h[:, kk], oT_l[:, kk])
                ins.then_inc(group_done, 1)
            pe.wait_ge(m_ready, KD)
            for g in range(G_OUT, G_END):
                pe.wait_ge(split_lo, g + 1)
                if g >= G_OUT + 2:
                    pe.wait_ge(x1_ready, g - G_OUT - 1)
                token_group((g - G_OUT) % 2 * 2, g % 2, mT_h, mT_l)

            pe.wait_ge(h2_ready, NB)
            for k in range(KD):
                if k >= 2:
                    pe.wait_ge(h2T_out[k % 2], k // 2)
                for c in range(NB):
                    ins = pe.transpose(ps[:, 4 + k % 2, c * P:(c + 1) * P], h2n[:, c, k * P:(k + 1) * P], ident[:, :])
                ins.then_inc(h2T_ps, 1)
            pe.wait_ge(h2T_out[0], KD // 2)
            pe.wait_ge(h2T_out[1], KD // 2)
            for c in range(NB):
                for k in range(KD):
                    ins = pe.matmul(ps[:, 6, c * E:(c + 1) * E], h2T[:, k, c * P:(c + 1) * P], w_rt[:, k, :],
                                    start=(k == 0), stop=(k == KD - 1))
            ins.then_inc(logits_ps, 1)
            pe.wait_ge(picked, 1)
            for c in range(NB):
                pe.matmul(ps[:, 4, 0:E], ones_b[:, :], sel_b[:, c, :], start=(c == 0), stop=(c == NB - 1))
            for c in range(NB):
                for c1 in range(c + 1):
                    ins = pe.matmul(ps[:, 7, c * E:(c + 1) * E], (before_b if c1 == c else ones_b)[:, :], sel_b[:, c1, :],
                                    start=(c1 == 0), stop=(c1 == c))
            ins.then_inc(place_ps, 1)
            pe.wait_ge(gates_ready, 1)
            pe.transpose(ps[:, 5, 0:P], r_gt[:, :, :].rearrange("p c e -> p (c e)"), ident[:, :]).then_inc(gateT_ps, 1)

            def lists(i, first=False):
                pe.wait_ge(sel_ready, i + 1)
                if not first:
                    pe.wait_ge(idx_ready, i)
                for c in range(NB):
                    rhs = row_tab[:, c, i, :] if isinstance(i, int) else \
                        row_tab[:, c, bass.ds(i, 1), :].rearrange("p a t -> p (a t)")
                    ins = pe.matmul(list_v, sel[:, c, :], rhs, start=(c == 0), stop=(c == NB - 1))
                ins.then_inc(list_ps, 1)

            def turn_rows(i, first=False):
                pe.wait_ge(xg_in, i * 16 + 16)
                if not first:
                    pe.wait_ge(xT_ready, i)
                for k in range(KD):
                    ins = pe.transpose(xT_ps_v[:, k], xg[:, k * P:(k + 1) * P], ident[0:SLOTS, 0:SLOTS])
                ins.then_inc(xT_ps, 1)

            def gate_up(i, first=False):
                pe.wait_ge(xT_ready, i + 1)
                if not first:
                    pe.wait_ge(gu_out, i)
                for k in range(KD):
                    pe.wait_ge(gu_in[k], i * 16 + 16)
                    for f in range(2 * KD):
                        ins = pe.matmul(gu_v[:, f], gu_chunk(k)[:, f * P:(f + 1) * P], xT[:, k, :],
                                        start=(k == 0 and f % 4 == 0), stop=(k == KD - 1), skip_group_check=True)
                    ins.then_inc(gu_used[k], 1)
                    if k == 1:
                        lists(i + 1)

            def down(n):
                pe.wait_ge(a_ready, n)
                pe.wait_ge(y_ready, n)
                for j in range(4):
                    pe.wait_ge(dn_lo[j], n)
                    for k in (0, 1):
                        f = 2 * j + k
                        a_h, a_l = aT_h[:, f, :], aT_l[:, f, :]
                        for half in (0, 1):
                            s = slice(half * 512, (half + 1) * 512)
                            w_h, w_l = wdn_h[:, j, k, s], wdn_l[:, j, k, s]
                            pe.matmul(ps[0:SLOTS, 4 + half, :], a_h, w_h, start=(f == 0), stop=False)
                            pe.matmul(ps[0:SLOTS, 4 + half, :], a_h, w_l, start=False, stop=False)
                            ins = pe.matmul(ps[0:SLOTS, 4 + half, :], a_l, w_h, start=False, stop=(f == KD - 1))
                    ins.then_inc(dn_used[j], 1)

            lists(0, first=True)
            turn_rows(0, first=True)
            gate_up(0, first=True)
            turn_rows(1)
            pe.wait_ge(items_ready, 1)
            pe.wait_ge(gateT_ready, 1)
            pe.wait_ge(b_dn_in, 16 * NB)
            for m in range(8):
                c, n0 = m // 2, m % 2 * 512
                if m >= 2:
                    pe.wait_ge(bdn_out, m - 1)
                pe.matmul(ps[:, 4 + m % 2, :], gateT[c * E:(c + 1) * E, :], b_dn[c * E:(c + 1) * E, n0:n0 + 512],
                          start=True, stop=True).then_inc(bdn_ps, 1)
            n_items = pe.value_load(items[0:1, N_AT:N_AT + 1], min_val=E, max_val=E + MAX_EXTRA)
            with pe.Fori(1, n_items) as i:
                gate_up(i)
                turn_rows(i + 1)
                down(i)
            down(n_items)


_INS = ["x", "positions", "norm1_g", "w_in", "b_forget", "b_gate", "q_norm_swa", "k_norm_swa", "sinks",
        "q_norm_fox", "k_norm_fox", "w_o_swa", "w_o_fox", "w_out", "norm2_g", "w_router", "b_router",
        "w_gate_up", "b_gate_up", "w_down", "b_down"]


def kernel(**inputs):
    import numpy as _np
    import concourse.bacc as _bacc
    from concourse.bass_utils import run_bass_kernel_spmd as _run

    nc = _bacc.Bacc("TRN2", target_bir_lowering=False, num_devices=1)
    arrays, args = {}, []
    for name in _INS:
        a = _np.ascontiguousarray(inputs[name])
        arrays[f"in_{name}_dram"] = a
        args.append(nc.dram_tensor(f"in_{name}_dram", a.shape, mybir.dt.from_np(a.dtype), kind="ExternalInput").ap())
    args.append(nc.dram_tensor("out_0_dram", inputs["x"].shape, F32, kind="ExternalOutput").ap())
    hybrid_block(nc, *args)
    r = _run(nc, [arrays], core_ids=[0])
    return r.results[0]["out_0_dram"]
```

```python
from contextlib import ExitStack

import numpy as np

import concourse.bass as bass
from concourse import mybir

F32 = mybir.dt.float32
F32R = mybir.dt.float32r
BF16 = mybir.dt.bfloat16
I32 = mybir.dt.int32
ALU = mybir.AluOpType
ACT = mybir.ActivationFunctionType
AX = mybir.AxisListType

P = 128
HD = 64
ROPE_THETA = 10000.0
TOP_K = 4
LIMIT = 7.0
ALPHA = 1.702
EPS = 1e-6
NEG = -1e30
SCALE = HD ** -0.5
GW = 256
SLOTS = 96
MAGIC = 12582912.0
TWO_PI = 2.0 * np.pi
C1 = 6.28125
C2 = float(np.float32(np.floor((TWO_PI - C1) * 2 ** 21) / 2 ** 21))
C3 = float(np.float32(TWO_PI - C1 - C2))


def bc(ap, axis, n):
    new = ap.unsqueeze(axis)
    shape = list(new.shape)
    shape[axis] = n
    return new.broadcast_to(shape)


def hybrid_block(nc, x, positions, norm1_g, w_in, b_forget, b_gate, q_norm_swa, k_norm_swa, sinks,
                 q_norm_fox, k_norm_fox, w_o_swa, w_o_fox, w_out, norm2_g, w_router, b_router,
                 w_gate_up, b_gate_up, w_down, b_down, out):
    T, D = x.shape[1:]
    NB, KD = T // P, D // P
    HF = b_forget.shape[1]
    HQ = sinks.shape[1]
    QW, FW = HQ * HD, HF * HD
    KV = (w_in.shape[2] - QW - 3 * FW - HF - 2 * D) // (2 * HD)
    KVW = KV * HD
    QKV = QW + 2 * KVW + 3 * FW
    E, F = w_gate_up.shape[1], w_down.shape[2]
    F2 = 2 * F
    assert (NB, KD, HQ, HF, KV, E, F, QKV) == (4, 8, 8, 8, 2, 32, 1024, 2304)
    KA, VA, QF = QW, QW + KVW, QW + 2 * KVW
    KF, VF = QF + FW, QF + 2 * FW
    FL, GATE = QKV, QKV + HF
    SWA_H, FOX_H = HQ + KV, 2 * HF

    N_QKV, N_GATE, N_O, N_OUT = QKV // GW, 2 * D // GW, D // GW, D // GW
    G_GATE, G_O = N_QKV, N_QKV + N_GATE
    G_OUT = G_O + N_O
    G_END = G_OUT + N_OUT

    MAX_EXTRA = T * TOP_K // SLOTS
    LEVELS = -(-T // SLOTS) - 1
    ITEMS = E + MAX_EXTRA + 2
    N_AT, LAST_AT = 63, 62

    stage_waits = []
    total = [0, 0]
    for g in range(G_END):
        total[g % 2] += 32 if G_O <= g < G_OUT else 16
        stage_waits.append(total[g % 2])

    with ExitStack() as ctx:
        base = (nc.sbuf_base + 63) // 64 * 64

        class Region:
            top = base

            def __init__(self, size):
                self.start, self.end = Region.top, Region.top + size
                self.at = self.start
                Region.top = self.end
                assert self.end <= nc.sbuf_usable_end, (self.end, nc.sbuf_usable_end)

            def rewind(self, offset=0):
                self.at = self.start + offset

            def put(self, name, shape, dt=F32):
                size = int(np.prod(shape[1:])) * (2 if dt == BF16 else 4)
                t = nc.alloc_sbuf_tensor_at(name, shape, dt, offset=self.at)
                self.at += (size + 31) // 32 * 32
                assert self.at <= self.end, (name, self.at - self.end)
                return t

        K = 1024
        stage, hold = Region(48 * K), Region(48 * K)
        xreg, r1, r2, work, const = Region(16 * K), Region(32 * K), Region(36 * K), Region(10 * K), Region(17 * K)

        st_w = stage.put("st_w", [P, 2, KD, GW])
        st_h = stage.put("st_h", [P, 2, KD, GW], F32R)
        st_l = stage.put("st_l", [P, 2, KD, GW], F32R)
        stage.rewind()
        gu_tail = stage.put("gu_tail", [P, 2, F2])
        wdn = stage.put("wdn", [P, 4, 2, D])
        stage.rewind(16 * K)
        wdn_l = stage.put("wdn_l", [P, 4, 2, D], F32R)
        stage.rewind()
        gu_tail_l = stage.put("gu_tail_l", [P, 2, F2], F32R)
        gates_T = hold.put("gates_T", [P, 2 * KD, T])
        o_tok = hold.put("o_tok", [P, NB, QW + FW])
        hold.rewind()
        gu_head = hold.put("gu_head", [P, 6, F2])
        hold.rewind()
        gu_head_l = hold.put("gu_head_l", [P, 6, F2], F32R)
        hold.rewind()
        hn_tok = hold.put("hn_tok", [P, NB, D])
        bgu_rows = hold.put("bgu_rows", [E, F2])
        vec_rows = hold.put("vec_rows", [32, P])
        wfl = hold.put("wfl", [P, KD, 32])
        wfl_hl = hold.put("wfl_hl", [P, KD, 64], F32R)
        flT = hold.put("flT", [64, T])
        assert hold.at <= hold.start + 32 * K
        hold.rewind(32 * K)
        k_dup = hold.put("k_dup", [P, NB, KV, 2, HD])
        sq = hold.put("sq", [P, (SWA_H + FOX_H) * HD])
        rot = hold.put("rot", [P, 2, SWA_H, HD])
        x_tok = xreg.put("x_tok", [P, NB, D])
        xreg.rewind()
        gu_hi = xreg.put("gu_hi", [P, 4, 2, F // 2], F32R)
        hT_h = r1.put("hT_h", [P, KD, T], F32R)
        hT_l = r1.put("hT_l", [P, KD, T], F32R)
        r1.rewind()
        qaT = r1.put("qaT", [P, HQ // 2, T])
        kaT = r1.put("kaT", [P, KV, T])
        qfT = r1.put("qfT", [P, HF // 2, T])
        kfT = r1.put("kfT", [P, HF // 2, T])
        r1.rewind()
        oT_h = r1.put("oT_h", [P, KD, T], F32R)
        oT_l = r1.put("oT_l", [P, KD, T], F32R)
        r1.rewind()
        h2T = r1.put("h2T", [P, KD, T])
        h2n = r1.put("h2n", [P, NB, D])
        tok = r2.put("tok", [P, NB, QKV])
        r2.rewind()
        mT_h = r2.put("mT_h", [P, KD, T], F32R)
        mT_l = r2.put("mT_l", [P, KD, T], F32R)
        r2.rewind()
        xg = r2.put("xg", [SLOTS, D])
        xT = r2.put("xT", [P, KD, SLOTS])
        act_g = r2.put("act_g", [P, KD, SLOTS])
        act_u = r2.put("act_u", [P, KD, SLOTS])
        act_s = r2.put("act_s", [P, KD, SLOTS])
        aT = r2.put("aT", [P, KD, SLOTS])
        r2.at -= KD * SLOTS * 4
        aT_l = r2.put("aT_l", [P, KD, SLOTS], F32R)
        ysb = r2.put("ysb", [SLOTS, D])
        sel = r2.put("sel", [P, NB, SLOTS], BF16)
        zero_rows = r2.put("zero_rows", [SLOTS, D])
        r2.at -= D * 4
        gu_tok = r2.put("gu_tok", [SLOTS, 2, F // 2])
        c_hi = work.put("c_hi", [P, T], F32R)
        lf = work.put("lf", [P, NB, P])
        ang = work.put("ang", [P, NB, HD // 2])
        ang_k = work.put("ang_k", [P, NB, HD // 2])
        sin_t = work.put("sin_t", [P, NB, HD // 2])
        cos_t = work.put("cos_t", [P, NB, HD // 2])
        rope_c = work.put("rope_c", [P, 2, NB, HD])
        rope_s = work.put("rope_s", [P, 2, NB, HD])
        work.rewind()
        p_sb = work.put("p_sb", [P, 3, T])
        pT_sb = work.put("pT_sb", [P, 2, T])
        work.rewind()
        merge_t = work.put("merge_t", [P, 2, T])
        merge_s = work.put("merge_s", [P, 2, T])
        work.rewind()
        b_dn = work.put("b_dn", [P, D])
        gateT = work.put("gateT", [P, P])
        lg = work.put("lg", [P, NB, E])
        r_gt = work.put("r_gt", [P, NB, E])
        r_eq = work.put("r_eq", [P, NB, E])
        r_in = work.put("r_in", [P, NB, E])
        r_ex = work.put("r_ex", [P, NB, E])
        aT_h = work.put("aT_h", [P, KD, SLOTS], F32R)
        work.rewind()
        xT_h = work.put("xT_h", [P, KD, SLOTS], F32R)
        xT_l = work.put("xT_l", [P, KD, SLOTS], F32R)
        HN = SWA_H + FOX_H
        ident = const.put("ident", [P, P])
        ident_b = const.put("ident_b", [P, P], BF16)
        mask_b = const.put("mask_b", [P, 2, P], BF16)
        upto = const.put("upto", [P, T])
        before_b = const.put("before_b", [P, P], BF16)
        ones_b = const.put("ones_b", [P, P], BF16)
        iota_i = const.put("iota_i", [P, P], I32)
        iota_f = const.put("iota_f", [P, P])
        tok_i = const.put("tok_i", [P, NB], I32)
        tok_f = const.put("tok_f", [P, NB])
        spare = const.put("spare", [P, 1])
        zeros = const.put("zeros", [P, ITEMS])
        inv = const.put("inv", [P, HD // 2])
        vcol = const.put("vcol", [P, 32])
        bgu = const.put("bgu", [P, E, 2 * KD])
        c_rows = const.put("c_rows", [P, T], F32R)
        c_pick = const.put("c_pick", [P, HF])
        c_pick_r = const.put("c_pick_r", [P, HF], F32R)
        ssq = const.put("ssq", [P, 2, NB])
        rstd = const.put("rstd", [P, 2, NB])
        hs_sum = const.put("hs_sum", [P, NB, HN])
        hs_r = const.put("hs_r", [P, NB, HN])
        minus_half = const.put("minus_half", [P, NB, HN])
        fl = const.put("fl", [P, NB, HF])
        fl_a = const.put("fl_a", [P, NB, HF])
        bf_bc = const.put("bf_bc", [P, HF])
        sink_bc = const.put("sink_bc", [P, HQ])
        sink8 = const.put("sink8", [P, HQ])
        brt = const.put("brt", [P, E])
        w_rt = const.put("w_rt", [P, KD, E])
        g_sw = const.put("g_sw", [P, 2, HD])
        g_fx = const.put("g_fx", [P, 2])
        pos_i = const.put("pos_i", [P, NB], I32)
        pos_f = const.put("pos_f", [P, NB])
        mx = const.put("mx", [P, 64])
        nb = const.put("nb", [P, 64])
        den = const.put("den", [P, 64])
        rden = const.put("rden", [P, 64])
        snk = const.put("snk", [P, HQ])
        ssq_g = const.put("ssq_g", [P, N_OUT, NB])
        top8 = r2.put("top8", [P, NB, 8])
        need = r2.put("need", [P, NB])
        zsum = r2.put("zsum", [P, NB])
        sel_b = r2.put("sel_b", [P, NB, E], BF16)
        slot_tab = r2.put("slot_tab", [P, NB, ITEMS])
        row_tab = r2.put("row_tab", [P, NB, ITEMS, 5], BF16)
        row_f = r2.put("row_f", [SLOTS, 1])
        cnt = r2.put("cnt", [P, E])
        ext = r2.put("ext", [P, E])
        ext_in = r2.put("ext_in", [P, E])
        ext_ex = r2.put("ext_ex", [P, E])
        item_e = r2.put("item_e", [P, MAX_EXTRA])
        item_b = r2.put("item_b", [P, MAX_EXTRA])
        items_f = r2.put("items_f", [1, 64])
        items = r2.put("items", [1, 64], I32)
        idx_g = r2.put("idx_g", [SLOTS, 1], I32)
        idx_s = r2.put("idx_s", [SLOTS, 1], I32)
        idx_all = r2.put("idx_all", [SLOTS, ITEMS], I32)
        gate_all = r2.put("gate_all", [SLOTS, ITEMS])
        r1.rewind()
        onehot = r1.put("onehot", [P, MAX_EXTRA, E])
        onehot_t = r1.put("onehot_t", [P, MAX_EXTRA, E])
        r1.rewind()
        wdn_h = r1.put("wdn_h", [P, 4, 2, D], F32R)

        ps = ctx.enter_context(nc.psum_tensor("ps", [P, 8, 512], F32))
        xT_ps_v = ps[:, 6:8, :].rearrange("p b (k s) -> p (b k) s", k=4)[:, :, 0:SLOTS]
        list_v = ps[0:SLOTS, 6, SLOTS:SLOTS + 5]
        gu_v = ps[:, 0:4, :].rearrange("p b (k s) -> p (b k) s", k=4)[:, :, 0:SLOTS]
        h2_dram = nc.dram_tensor("h2_dram", (T, D), F32, kind="Internal").ap()
        acc_dram = nc.dram_tensor("acc_dram", (T + SLOTS, D), F32, kind="Internal").ap()
        BIG = 8.0 * T

        x_v = x[0].rearrange("(c p) d -> p c d", p=P)
        w_in_v = w_in[0].rearrange("(k p) n -> p k n", p=P)
        w_oa_v = w_o_swa[0].rearrange("(k p) n -> p k n", p=P)
        w_ob_v = w_o_fox[0].rearrange("(k p) n -> p k n", p=P)
        w_out_v = w_out[0].rearrange("(k p) n -> p k n", p=P)
        w_gu_v = w_gate_up.rearrange("l e (k p) n -> (l e) k p n", p=P)
        w_dn_v = w_down.rearrange("l e (j k p) n -> (l e) j p k n", p=P, k=2)

        def sem(name):
            return ctx.enter_context(nc.semaphore(name))

        x_in = [sem(f"x_in{c}") for c in range(NB)]
        rows_in, small_in, wfl_in = sem("rows_in"), sem("small_in"), sem("wfl_in")
        stage_in = [sem("stage_in0"), sem("stage_in1")]
        b_dn_in = sem("b_dn_in")
        gu_in = [sem(f"gu_in{k}") for k in range(KD)]
        dn_in = [sem(f"dn_in{j}") for j in range(4)]
        last_dn_in = [sem(f"last_dn_in{j}") for j in range(4)]
        pool_step, dve_step = sem("pool_step"), sem("dve_step")
        consts, ident_done, squared = sem("consts"), sem("ident_done"), sem("squared")
        var_ready, rstd_ready, hn_ready = sem("var_ready"), sem("rstd_ready"), sem("hn_ready")
        hT_ps, hT_hi, hT_ready = sem("hT_ps"), sem("hT_hi"), sem("hT_ready")
        rows_ps, vcol_ready, bgu_ready = sem("rows_ps"), sem("vcol_ready"), sem("bgu_ready")
        split_hi, split_lo = sem("split_hi"), sem("split_lo")
        group_done, group_out = sem("group_done"), sem("group_out")
        wfl_hi, wfl_ready, fl_ps = sem("wfl_hi"), sem("wfl_ready"), sem("fl_ps")
        flT_ps, flT_ready = sem("flT_ps"), sem("flT_ready")
        fl_abs, fl_exp, fl_ln = sem("fl_abs"), sem("fl_exp"), sem("fl_ln")
        lf_ready, c_ps, c_hi_ready, c_ready = sem("lf_ready"), sem("c_ps"), sem("c_hi_ready"), sem("c_ready")
        heads_sq, sq_read, hs_var, hs_rstd = sem("heads_sq"), sem("sq_read"), sem("hs_var"), sem("hs_rstd")
        ang_ready, sin_ready, qk_ready = sem("ang_ready"), sem("sin_ready"), sem("qk_ready")
        qkT_ps, qkT_out = sem("qkT_ps"), [sem("qkT_out0"), sem("qkT_out1")]
        scores, maxed, shift, probs = sem("scores"), sem("maxed"), sem("shift"), sem("probs")
        pT_ps, pT_ready, pv_done = sem("pT_ps"), sem("pT_ready"), sem("pv_done")
        snk_in, snk_exp, o_out = sem("snk_in"), sem("snk_exp"), sem("o_out")
        oT_ps, oT_hi, oT_ready = sem("oT_ps"), sem("oT_hi"), sem("oT_ready")
        half_done = sem("half_done")
        m_part, m_sum, m_hi, m_ready = sem("m_part"), sem("m_sum"), sem("m_hi"), sem("m_ready")
        x1_ready, x1_squared, x1_sum = sem("x1_ready"), sem("x1_squared"), sem("x1_sum")
        h2_ready, h2_stored = sem("h2_ready"), sem("h2_stored")
        h2T_ps, h2T_out = sem("h2T_ps"), [sem("h2T_out0"), sem("h2T_out1")]
        logits_ps, r_shifted, r_exp, picked = sem("logits_ps"), sem("r_shifted"), sem("r_exp"), sem("picked")
        place_ps, gates_ready, gateT_ps, gateT_ready = (sem("place_ps"), sem("gates_ready"), sem("gateT_ps"),
                                                        sem("gateT_ready"))
        bdn_ps, bdn_out, spare_set = sem("bdn_ps"), sem("bdn_out"), sem("spare_set")
        acc_set = [sem(f"acc_set{c}") for c in range(NB)]
        items_ready, zero_ready = sem("items_ready"), sem("zero_ready")
        row_sum = sem("row_sum")
        sel_ready, list_ps, idx_ready, xg_in = sem("sel_ready"), sem("list_ps"), sem("idx_ready"), sem("xg_in")
        xT_ps, xT_ready = sem("xT_ps"), sem("xT_ready")
        gu_used = [sem(f"gu_used{k}") for k in range(KD)]
        g_biased, gu_out, g_ready, u_ready = sem("g_biased"), sem("gu_out"), sem("g_ready"), sem("u_ready")
        sig_ready, gs_ready, a_whole = sem("sig_ready"), sem("gs_ready"), sem("a_whole")
        a_hi, a_ready = sem("a_hi"), sem("a_ready")
        xT_hi, xT_split = sem("xT_hi"), sem("xT_split")
        rows_done, rows_kept, gu_turned = sem("rows_done"), sem("rows_kept"), sem("gu_turned")
        gu_hi_done, gu_split = sem("gu_hi_done"), sem("gu_split")
        dn_hi, dn_lo = sem("dn_hi"), sem("dn_lo")
        dn_used = [sem(f"dn_used{j}") for j in range(4)]
        idx_s_ready, added, turn = sem("idx_s_ready"), sem("added"), sem("turn")
        y_ready, y_free = sem("y_ready"), sem("y_free")
        out_done = sem("out_done")

        def gu_chunk(k):
            return gu_head[:, k, :] if k < 6 else gu_tail[:, k - 6, :]

        def split_columns(chunk):
            return chunk.rearrange("p (a b n) -> p a b n", a=2, b=2)[:, :, 1, :]

        def gu_low(k):
            return split_columns(gu_head_l[:, k, :] if k < 6 else gu_tail_l[:, k - 6, :])

        units = [(c, b, h) for c in range(NB) for b in (0, 1) for h in range(8)]
        NU = len(units)
        QKT = [(s, j) for s in range(4) for j in range((HQ // 2, KV, HF // 2, HF // 2)[s])]

        QKT_BANK = (4, 5, 2, 3)

        def width(n):
            c, fox, _ = units[n]
            return (c + 1) * P if fox else min(c + 1, 2) * P

        block = ctx.enter_context(nc.Block())

        @block.sync
        def _(sp):
            for c in range(NB):
                sp.dma_start(x_tok[:, c, :], x_v[:, c, :]).then_inc(x_in[c], 16)

            for g in range(G_END):
                if g >= 2:
                    sp.wait_ge(split_lo, g - 1)
                dst, s = st_w[:, g % 2], stage_in[g % 2]
                if g < G_O:
                    c0 = g * GW if g < G_GATE else GATE + (g - G_GATE) * GW
                    sp.dma_start(dst, w_in_v[:, :, c0:c0 + GW]).then_inc(s, 16)
                elif g < G_OUT:
                    c0 = (g - G_O) * GW
                    sp.dma_start(dst[:, 0:4], w_oa_v[:, :, c0:c0 + GW]).then_inc(s, 16)
                    sp.dma_start(dst[:, 4:8], w_ob_v[:, :, c0:c0 + GW]).then_inc(s, 16)
                else:
                    c0 = (g - G_OUT) * GW
                    sp.dma_start(dst, w_out_v[:, :, c0:c0 + GW]).then_inc(s, 16)
                if g == 0:
                    sp.dma_start(wfl[:, :, 0:HF], w_in_v[:, :, FL:FL + HF]).then_inc(wfl_in, 16)
                if g == 1:
                    sp.dma_start(bf_bc[:, :], b_forget[0].partition_broadcast(P)).then_inc(small_in, 16)
                    sp.dma_start(sink_bc[:, :], sinks[0].partition_broadcast(P)).then_inc(small_in, 16)
                    sp.dma_start(brt[:, :], b_router[0].partition_broadcast(P)).then_inc(small_in, 16)
                    sp.dma_start(g_sw[:, 0, :], q_norm_swa[0].partition_broadcast(P)).then_inc(small_in, 16)
                    sp.dma_start(g_sw[:, 1, :], k_norm_swa[0].partition_broadcast(P)).then_inc(small_in, 16)
                    sp.dma_start(w_rt[:, :, :], w_router[0].rearrange("(k p) e -> p k e", p=P)).then_inc(small_in, 16)
                    with nc.allow_non_contiguous_dma(reason="a few hundred words onto partitions"):
                        sp.dma_start(pos_i[:, :], positions[0].rearrange("(c p) -> p c", p=P)).then_inc(small_in, 16)
                        for a, w in enumerate((q_norm_fox, k_norm_fox)):
                            for half in (0, 1):
                                sp.dma_start(g_fx[half * HD:(half + 1) * HD, a:a + 1],
                                             w[0].rearrange("(d o) -> d o", o=1)).then_inc(small_in, 16)

            def load_gu(e, k):
                src = w_gu_v[e, k] if isinstance(e, int) else w_gu_v[bass.ds(e, 1), k].rearrange("a p n -> (a p) n")
                sp.dma_start(gu_chunk(k), src).then_inc(gu_in[k], 16)

            def load_dn(e, j):
                src = w_dn_v[e, j] if isinstance(e, int) else w_dn_v[bass.ds(e, 1), j].rearrange("a p k n -> (a p) k n")
                sp.dma_start(wdn[:, j, :, :], src).then_inc(dn_in[j], 16)

            sp.wait_ge(m_sum, KD)
            for k in range(6):
                load_gu(0, k)
            sp.wait_ge(split_lo, G_END)
            for k in range(6, KD):
                load_gu(0, k)
            sp.wait_ge(group_done, G_END)
            for j in (0, 1):
                load_dn(0, j)
            for c in range(NB):
                sp.dma_start(b_dn[c * E:(c + 1) * E, :], b_down[0]).then_inc(b_dn_in, 16)
            for c in range(NB):
                sp.wait_ge(h2_ready, c + 1)
                sp.dma_start(h2_dram[c * P:(c + 1) * P, :], h2n[:, c, :]).then_inc(h2_stored, 16)
            for j in (2, 3):
                sp.wait_ge(xg_in, 16)
                load_dn(0, j)
            for k in range(KD):
                sp.wait_ge(gu_used[k], 1)
                load_gu(1, k)
            sp.wait_ge(items_ready, 1)
            last = sp.value_load(items[0:1, LAST_AT:LAST_AT + 1], min_val=E - 1, max_val=E + MAX_EXTRA - 1)
            with sp.Fori(1, last) as i:
                e1 = sp.value_load(items[0:1, bass.ds(i + 1, 1)], min_val=0, max_val=E - 1)
                e = sp.value_load(items[0:1, bass.ds(i, 1)], min_val=0, max_val=E - 1)
                for k in range(KD):
                    sp.wait_ge(gu_used[k], i + 1)
                    load_gu(e1, k)
                for j in range(4):
                    sp.wait_ge(dn_used[j], i)
                    load_dn(e, j)
            e = sp.value_load(items[0:1, bass.ds(last, 1)], min_val=0, max_val=E - 1)
            for j in range(4):
                sp.wait_ge(gu_used[j], last + 1)
                sp.dma_start(gu_head[:, j, :].rearrange("p (k n) -> p k n", k=2),
                             w_dn_v[bass.ds(e, 1), j].rearrange("a p k n -> (a p) k n")).then_inc(last_dn_in[j], 16)
            sp.wait_ge(y_free, last + 2)
            sp.dma_start(out[0], acc_dram[0:T, :]).then_inc(out_done, 16)
            sp.wait_ge(out_done, 16)

        @block.gpsimd
        def _(pool):
            steps = [0]

            def then(ins):
                steps[0] += 1
                ins.then_inc(pool_step, 1)
                pool.wait_ge(pool_step, steps[0])

            g = nc.gpsimd
            then(g.memset(ident[:, :], 0.0))
            then(g.affine_select(out=ident[:, :], in_=ident[:, :], compare_op=ALU.not_equal, fill=1.0,
                                 base=0, pattern=[[-1, P]], channel_multiplier=1))
            g.tensor_copy(ident_b[:, :], ident[:, :]).then_inc(ident_done, 1)
            g.memset(minus_half[:, :, :], -0.5)
            g.memset(wfl[:, :, HF:], 0.0)
            g.memset(lf[:, :, :], 0.0)
            g.memset(zeros[:, :], 0.0)
            for j in range(HD // 2):
                g.memset(inv[:, j:j + 1], float(np.float32(ROPE_THETA ** (-j / (HD // 2)))))
            g.memset(upto[:, :], 1.0)
            g.memset(before_b[:, :], 1.0)
            g.memset(ones_b[:, :], 1.0)
            g.memset(c_pick[:, :], 0.0)
            then(g.memset(mask_b[:, :, :], 0.0))
            g.affine_select(out=upto[:, 0:P], in_=upto[:, 0:P], compare_op=ALU.is_ge, fill=0.0,
                            base=0, pattern=[[1, P]], channel_multiplier=-1)
            g.affine_select(out=before_b[:, :], in_=before_b[:, :], compare_op=ALU.is_gt, fill=0.0,
                            base=0, pattern=[[1, P]], channel_multiplier=-1)
            g.affine_select(out=mask_b[:, 0, :], in_=mask_b[:, 0, :], compare_op=ALU.is_gt, fill=NEG,
                            base=0, pattern=[[1, P]], channel_multiplier=-1)
            g.affine_select(out=mask_b[:, 1, :], in_=mask_b[:, 1, :], compare_op=ALU.is_ge, fill=NEG,
                            base=0, pattern=[[-1, P]], channel_multiplier=1)
            for row in range(0, P, 32):
                then(g.affine_select(out=c_pick[:, :], in_=c_pick[:, :], compare_op=ALU.not_equal, fill=1.0,
                                     base=-row, pattern=[[-1, HF]], channel_multiplier=1))
            g.tensor_copy(c_pick_r[:, :], c_pick[:, :])
            g.iota(iota_i[:, :], pattern=[[1, P]], base=0, channel_multiplier=0)
            then(g.iota(tok_i[:, :], pattern=[[P, NB]], base=0, channel_multiplier=1))
            g.tensor_copy(iota_f[:, :], iota_i[:, :])
            then(g.tensor_copy(tok_f[:, :], tok_i[:, :]))
            g.tensor_scalar(spare[:, :], tok_f[:, 0:1], float(T), None, ALU.add).then_inc(consts, 1)

            pool.wait_ge(var_ready, 1)
            g.tensor_tensor(rstd[:, 0, :], ssq[:, 0, :], minus_half[:, 0, 0:NB], ALU.pow).then_inc(rstd_ready, 1)
            for c in range(NB):
                pool.wait_ge(hs_var, c + 1)
                g.tensor_tensor(hs_r[:, c, :], hs_sum[:, c, :], minus_half[:, c, :], ALU.pow).then_inc(hs_rstd, 1)
            pool.wait_ge(group_done, G_END)
            g.memset(zero_rows[:, :], 0.0).then_inc(zero_ready, 1)
            pool.wait_ge(var_ready, 2)
            g.tensor_tensor(rstd[:, 1, :], ssq[:, 1, :], minus_half[:, 0, 0:NB], ALU.pow).then_inc(rstd_ready, 1)

            def gather():
                g.indirect_dma_start(out=xg[:, :], out_offset=None, in_=h2_dram[:, :],
                                     in_offset=bass.IndirectOffsetOnAxis(ap=idx_g[:, :], axis=0)).then_inc(xg_in, 16)

            def add_rows(n, column):
                pool.wait_ge(consts, 1)
                pool.wait_ge(y_ready, n + 1)
                g.tensor_copy(idx_s[:, :], idx_all[:, column]).then_inc(idx_s_ready, 1)
                pool.wait_ge(spare_set, 16)
                pool.wait_ge(idx_s_ready, n)
                g.indirect_dma_start(out=acc_dram[:, :],
                                     out_offset=bass.IndirectOffsetOnAxis(ap=idx_s[:, :], axis=0),
                                     in_=ysb[:, :], in_offset=None, compute_op=ALU.add).then_inc(added, 16)
                pool.wait_ge(added, n * 16)
                pool.sem_inc(y_free, 1)

            pool.sem_inc(y_free, 1)
            pool.wait_ge(h2_stored, 16 * NB)
            pool.wait_ge(idx_ready, 1)
            gather()
            pool.wait_ge(idx_ready, 2)
            pool.wait_ge(xT_ps, 1)
            gather()
            pool.wait_ge(idx_ready, 3)
            pool.wait_ge(xT_ps, 2)
            gather()
            pool.wait_ge(spare_set, 16)
            for c in range(NB):
                pool.wait_ge(acc_set[c], 16)
            pool.wait_ge(items_ready, 1)
            n_items = pool.value_load(items[0:1, N_AT:N_AT + 1], min_val=E, max_val=E + MAX_EXTRA)
            with pool.Fori(1, n_items) as i:
                pool.wait_ge(idx_ready, i + 3)
                pool.wait_ge(xT_ps, i + 2)
                pool.sem_inc(turn, 1)
                gather()
                add_rows(i, bass.ds(i - 1, 1))
            add_rows(n_items, bass.ds(n_items - 1, 1))

        @block.scalar
        def _(act):
            sc = nc.scalar
            act.dma_start(vec_rows[0:8, :], norm1_g[0].rearrange("(r c) -> r c", c=P)).then_inc(rows_in, 16)
            act.dma_start(vec_rows[8:16, :], norm2_g[0].rearrange("(r c) -> r c", c=P)).then_inc(rows_in, 16)
            act.dma_start(vec_rows[16:32, :], b_gate[0].rearrange("(r c) -> r c", c=P)).then_inc(rows_in, 16)
            act.dma_start(bgu_rows[:, :], b_gate_up[0]).then_inc(rows_in, 16)

            for c in range(NB):
                act.wait_ge(x_in[c], 16)
                sc.activation(hn_tok[:, c, :], x_tok[:, c, :], ACT.Square,
                              accum_out=ssq[:, 0, c:c + 1]).then_inc(squared, 1)

            def split_high(g):
                act.wait_ge(stage_in[g % 2], stage_waits[g])
                if g >= 2:
                    act.wait_ge(group_done, g - 1)
                sc.copy(st_h[:, g % 2], st_w[:, g % 2]).then_inc(split_hi, 1)

            split_high(0)
            act.wait_ge(wfl_in, 16)
            act.wait_ge(consts, 1)
            sc.copy(wfl_hl[:, :, 0:32], wfl[:, :, :]).then_inc(wfl_hi, 1)
            act.wait_ge(vcol_ready, 1)
            for k in range(KD):
                act.wait_ge(hT_ps, k + 1)
                sc.activation(hT_h[:, k, :], ps[:, k % 4, :], ACT.Identity,
                              scale=vcol[:, k:k + 1]).then_inc(hT_hi, 1)

            split_high(1)

            for g in range(G_GATE):
                if g >= 1:
                    split_high(g + 1)
                act.wait_ge(group_done, g + 1)
                sc.copy(tok[:, :, g * GW:(g + 1) * GW],
                        ps[:, g % 2 * 2:g % 2 * 2 + 2, :].rearrange("p b (c n) -> p (b c) n", c=2)).then_inc(group_out, 1)

            for g in range(G_GATE, G_O):
                c = g - G_GATE
                split_high(g + 1)
                if g == G_O - 1:
                    act.wait_ge(c_ps, 1)
                    sc.activation(c_hi[:, :], ps[:, 7, :], ACT.Copy, scale=-1.0 / SCALE)
                    for r in (0, 64):
                        ins = sc.activation(c_rows[r:r + 32, :], ps[r:r + 32, 7, :], ACT.Copy, scale=-1.0 / SCALE)
                    ins.then_inc(c_hi_ready, 1)
                if c < NB:
                    act.wait_ge(group_out, G_GATE)
                    if c >= 1:
                        act.wait_ge(sq_read, c)
                    sc.activation(sq[:, 0:SWA_H * HD], tok[:, c, 0:SWA_H * HD], ACT.Square)
                    sc.activation(sq[:, SWA_H * HD:], tok[:, c, QF:QF + FOX_H * HD], ACT.Square).then_inc(heads_sq, 1)
                if c == 0:
                    act.wait_ge(ang_ready, 1)
                    sc.activation(sin_t[:, :, :], ang[:, :, :], ACT.Sin)
                    sc.activation(cos_t[:, :, :], ang[:, :, :], ACT.Sin, scale=0.5).then_inc(sin_ready, 1)
                if c == 4:
                    act.wait_ge(fl_abs, 1)
                    sc.activation(fl_a[:, :, :], fl_a[:, :, :], ACT.Exp, scale=-1.0).then_inc(fl_exp, 1)
                    act.wait_ge(fl_exp, 1)
                    sc.activation(fl_a[:, :, :], fl_a[:, :, :], ACT.Ln, bias=1.0).then_inc(fl_ln, 1)
                act.wait_ge(group_done, g + 1)
                for d in (0, 1):
                    j = 2 * c + d
                    ins = sc.activation(gates_T[:, j, :], ps[:, g % 2 * 2 + d, :], ACT.Sigmoid,
                                        bias=vcol[:, 16 + j:17 + j])
                ins.then_inc(group_out, 1)
            sc.activation(snk[:, :], zeros[:, 0:HQ], ACT.Exp)
            for n in range(1, len(QKT), 2):
                s, j = QKT[n]
                act.wait_ge(qkT_ps, n + 1)
                dst, src = (qaT, kaT, qfT, kfT)[s][:, j, :], ps[:, QKT_BANK[n % 4], :]
                scale = 1.0 if s < 2 else g_fx[:, s - 2:s - 1]
                sc.activation(dst, src, ACT.Identity, scale=scale).then_inc(qkT_out[1], 1)

            for n in range(NU):
                act.wait_ge(shift, n + 1)
                if n >= 3:
                    act.wait_ge(pT_ps, n - 2)
                w = width(n)
                sc.activation(p_sb[:, n % 3, 0:w], ps[:, n % 4, 0:w], ACT.Exp, bias=nb[:, n:n + 1],
                              scale=SCALE, accum_out=den[:, n:n + 1]).then_inc(probs, 1)
                if n % 16 == 9:
                    act.wait_ge(snk_in, n // 16 + 1)
                    sc.activation(snk[:, :], snk[:, :], ACT.Exp).then_inc(snk_exp, 1)
            for k in range(KD):
                act.wait_ge(oT_ps, k + 1)
                sc.copy(oT_h[:, k, :], ps[:, k, :]).then_inc(oT_hi, 1)
            split_high(G_O + 1)
            for g in range(G_O, G_OUT):
                if g > G_O:
                    split_high(g + 1)
                for j in (2 * (g - G_O), 2 * (g - G_O) + 1):
                    act.wait_ge(m_sum, j + 1)
                    sc.copy(mT_h[:, j, :], merge_s[:, j % 2, :]).then_inc(m_hi, 1)

            def keep_odd(k):
                act.wait_ge(h2T_ps, k + 1)
                sc.activation(h2T[:, k, :], ps[:, 5, :], ACT.Identity,
                              scale=vcol[:, 8 + k:9 + k]).then_inc(h2T_out[1], 1)

            for m in range(N_OUT):
                if m + 1 < N_OUT:
                    split_high(G_OUT + m + 1)
                if m >= 1:
                    keep_odd(2 * m - 1)
                act.wait_ge(x1_ready, m + 1)
                for c in range(NB):
                    s = slice(m * GW, (m + 1) * GW)
                    ins = sc.activation(h2n[:, c, s], x_tok[:, c, s], ACT.Square, accum_out=ssq_g[:, m, c:c + 1])
                ins.then_inc(x1_squared, 1)
            keep_odd(KD - 1)
            act.wait_ge(rstd_ready, 2)
            for c in range(NB):
                sc.activation(h2n[:, c, :], x_tok[:, c, :], ACT.Identity, scale=rstd[:, 1, c:c + 1]).then_inc(h2_ready, 1)
                if c == 1:
                    act.wait_ge(r_shifted, 1)
                    sc.activation(r_ex[:, :, :], r_ex[:, :, :], ACT.Exp).then_inc(r_exp, 1)
            act.wait_ge(gateT_ps, 1)
            sc.copy(gateT[:, :], ps[:, 5, 0:P]).then_inc(gateT_ready, 1)

            def sigmoid(i, first=False):
                act.wait_ge(g_ready, i + 1)
                if not first:
                    act.wait_ge(gs_ready, i)
                sc.activation(act_s[:, :, :], act_g[:, :, :], ACT.Sigmoid, scale=ALPHA).then_inc(sig_ready, 1)

            def down_high(n, js=range(4)):
                for j in js:
                    act.wait_ge(consts, 1)
                    act.wait_ge(dn_in[j], n * 16)
                    sc.copy(wdn_h[:, j], wdn[:, j]).then_inc(dn_hi, 1)

            def act_high(i):
                act.wait_ge(a_whole, i + 1)
                sc.copy(aT_h[:, :, :], aT[:, :, :]).then_inc(a_hi, 1)

            def gate_up_high(n, ks):
                for k in ks:
                    act.wait_ge(consts, 1)
                    act.wait_ge(gu_in[k], n * 16 + 16)
                    if k >= 4:
                        act.wait_ge(gu_used[k - 4], n + 1)
                    elif not (isinstance(n, int) and n == 1):
                        act.wait_ge(gu_used[k + 4], n)
                    sc.copy(gu_hi[:, k % 4], split_columns(gu_chunk(k))).then_inc(gu_hi_done, 1)

            def rows_high(n):
                act.wait_ge(xT_ready, n + 1)
                sc.copy(xT_h[:, :, :], xT[:, :, :]).then_inc(xT_hi, 1)

            def keep_rows(i):
                act.wait_ge(rows_done, i)
                for half in (0, 1):
                    sc.copy(gu_tok[:, half, :], ps[0:SLOTS, 1 + 2 * half, :]).then_inc(rows_kept, 1)

            def weigh(n, column):
                act.wait_ge(consts, 1)
                act.wait_ge(dn_used[3], n)
                act.wait_ge(y_free, n)
                sc.activation(ysb[:, :].rearrange("p (b n) -> p b n", b=2), ps[0:SLOTS, 4:6, :], ACT.Identity,
                              scale=gate_all[:, column]).then_inc(y_ready, 1)

            act.wait_ge(zero_ready, 1)
            act.dma_start(acc_dram[T:T + SLOTS, :], zero_rows[:, :]).then_inc(spare_set, 16)
            for c in range(NB):
                act.wait_ge(bdn_out, 2 * c + 2)
                act.dma_start(acc_dram[c * P:(c + 1) * P, :], x_tok[:, c, :]).then_inc(acc_set[c], 16)
            act.sem_inc(gu_hi_done, KD)
            act.sem_inc(dn_hi, 4)
            for k in range(4):
                act.wait_ge(acc_set[k], 16)
                gate_up_high(1, (k,))
            rows_high(1)
            sigmoid(0, first=True)
            act_high(0)
            act.wait_ge(spare_set, 16)
            act.wait_ge(items_ready, 1)

            def act_item(i, ahead=True):
                for j in range(4):
                    down_high(i, (j,))
                    gate_up_high(i, (4 + j,))
                keep_rows(i)
                if ahead:
                    rows_high(i + 1)
                    gate_up_high(i + 1, range(4))
                sigmoid(i)
                if ahead:
                    act_high(i)
                weigh(i, bass.ds(i - 1, 1))

            last = act.value_load(items[0:1, LAST_AT:LAST_AT + 1], min_val=E - 1, max_val=E + MAX_EXTRA - 1)
            with act.Fori(1, last) as i:
                act_item(i)
            act_item(last, ahead=False)
            n_items = act.value_load(items[0:1, N_AT:N_AT + 1], min_val=E, max_val=E + MAX_EXTRA)
            weigh(n_items, bass.ds(n_items - 1, 1))

        @block.vector
        def _(dve):
            v = nc.vector
            steps = [0]

            def then(ins):
                steps[0] += 1
                ins.then_inc(dve_step, 1)
                dve.wait_ge(dve_step, steps[0])

            def split_low(g):
                dve.wait_ge(split_hi, g + 1)
                v.tensor_tensor(st_l[:, g % 2], st_w[:, g % 2], st_h[:, g % 2].bitcast(F32),
                                ALU.subtract).then_inc(split_lo, 1)

            dve.wait_ge(squared, NB)
            v.tensor_scalar(ssq[:, 0, :], ssq[:, 0, :], 1.0 / D, EPS, ALU.mult, ALU.add).then_inc(var_ready, 1)
            dve.wait_ge(rows_ps, 1)
            v.tensor_copy(vcol[:, :], ps[:, 6, 0:32]).then_inc(vcol_ready, 1)
            dve.wait_ge(rstd_ready, 1)
            for c in range(NB):
                v.tensor_scalar(hn_tok[:, c, :], x_tok[:, c, :], rstd[:, 0, c:c + 1], None, ALU.mult).then_inc(hn_ready, 1)
            split_low(0)
            dve.wait_ge(vcol_ready, 1)
            for k in range(KD):
                dve.wait_ge(hT_hi, k + 1)
                v.scalar_tensor_tensor(out=hT_l[:, k, :], in0=ps[:, k % 4, :], scalar=vcol[:, k:k + 1],
                                       in1=hT_h[:, k, :].bitcast(F32), op0=ALU.mult,
                                       op1=ALU.subtract).then_inc(hT_ready, 1)
            split_low(1)
            dve.wait_ge(wfl_hi, 1)
            v.tensor_tensor(wfl_hl[:, :, 32:64], wfl[:, :, :], wfl_hl[:, :, 0:32].bitcast(F32),
                            ALU.subtract).then_inc(wfl_ready, 1)
            dve.wait_ge(rows_ps, 2)
            v.tensor_copy(bgu[:, :, :].rearrange("p e j -> p j e"),
                          ps[:, 7, :].rearrange("p (j e) -> p j e", e=E)).then_inc(bgu_ready, 1)
            dve.wait_ge(consts, 1)
            dve.wait_ge(small_in, 16 * 11)
            then(v.tensor_copy(pos_f[:, :], pos_i[:, :]))
            then(v.tensor_tensor(ang[:, :, :], bc(pos_f[:, :], 2, HD // 2), bc(inv[:, :], 1, NB), ALU.mult))
            then(v.tensor_scalar(ang_k[:, :, :], ang[:, :, :], float(1.0 / TWO_PI), MAGIC, ALU.mult, ALU.add))
            then(v.tensor_scalar(ang_k[:, :, :], ang_k[:, :, :], -MAGIC, None, ALU.add))
            for part in (C1, C2, C3):
                then(v.scalar_tensor_tensor(out=ang[:, :, :], in0=ang_k[:, :, :], scalar=-part, in1=ang[:, :, :],
                                            op0=ALU.mult, op1=ALU.add))
            v.tensor_scalar(ang[:, :, :], ang[:, :, :], 3.1415925, -3.1415925, ALU.min, ALU.max).then_inc(ang_ready, 1)
            v.tensor_scalar(sink8[:, :], sink_bc[:, :], 1.0 / SCALE, None, ALU.mult)
            for g in range(2, G_GATE + 1):
                split_low(g)
                if g == G_GATE:
                    dve.wait_ge(flT_ps, 1)
                    v.tensor_copy(flT[:, :], ps[0:64, 6, :]).then_inc(flT_ready, 1)

            dve.wait_ge(fl_ps, 1)
            then(v.tensor_tensor(fl[:, :, :], ps[:, 6, 0:NB * HF].rearrange("p (c h) -> p c h", c=NB),
                                 bc(bf_bc[:, :], 1, NB), ALU.add))
            v.scalar_tensor_tensor(out=fl_a[:, :, :], in0=fl[:, :, :], scalar=-1.0, in1=fl[:, :, :],
                                   op0=ALU.mult, op1=ALU.max).then_inc(fl_abs, 1)

            heads_a = [tok[:, c, 0:SWA_H * HD].rearrange("p (h d) -> p h d", d=HD) for c in range(NB)]
            heads_f = [tok[:, c, QF:QF + FOX_H * HD].rearrange("p (h d) -> p h d", d=HD) for c in range(NB)]
            for g in range(G_GATE, G_O):
                c = g - G_GATE
                split_low(g + 1)
                if c < NB:
                    dve.wait_ge(heads_sq, c + 1)
                    v.tensor_reduce(hs_sum[:, c, :], sq[:, :].rearrange("p (h d) -> p h d", d=HD),
                                    AX.X, ALU.add).then_inc(sq_read, 1)
                    dve.wait_ge(sq_read, c + 1)
                    v.tensor_scalar(hs_sum[:, c, :], hs_sum[:, c, :], 1.0 / HD, EPS, ALU.mult, ALU.add).then_inc(hs_var, 1)
                if c == 1:
                    dve.wait_ge(sin_ready, 1)
                    then(v.tensor_tensor(cos_t[:, :, :], cos_t[:, :, :], cos_t[:, :, :], ALU.mult))
                    then(v.tensor_scalar(cos_t[:, :, :], cos_t[:, :, :], -2.0, 1.0, ALU.mult, ALU.add))
                    H2 = HD // 2
                    for a in (0, 1):
                        g1, g2 = bc(g_sw[:, a, 0:H2], 1, NB), bc(g_sw[:, a, H2:HD], 1, NB)
                        v.tensor_tensor(rope_c[:, a, :, 0:H2], cos_t[:, :, :], g1, ALU.mult)
                        v.tensor_tensor(rope_c[:, a, :, H2:HD], cos_t[:, :, :], g2, ALU.mult)
                        v.tensor_tensor(rope_s[:, a, :, H2:HD], sin_t[:, :, :], g1, ALU.mult)
                        then(v.scalar_tensor_tensor(out=rope_s[:, a, :, 0:H2], in0=sin_t[:, :, :], scalar=-1.0,
                                                    in1=g2, op0=ALU.mult, op1=ALU.mult))
                if 2 <= c < NB + 2:
                    c -= 2
                    dve.wait_ge(hs_rstd, c + 1)
                    v.tensor_tensor(heads_f[c], heads_f[c], bc(hs_r[:, c, SWA_H:HN], 2, HD), ALU.mult)
                    then(v.tensor_tensor(heads_a[c], heads_a[c], bc(hs_r[:, c, 0:SWA_H], 2, HD), ALU.mult))
                    for a, h0, h1 in ((0, 0, HQ), (1, HQ, SWA_H)):
                        n = h1 - h0
                        v.tensor_tensor(rot[:, 0, h0:h1, :], heads_a[c][:, h0:h1, :], bc(rope_c[:, a, c, :], 1, n), ALU.mult)
                        v.tensor_tensor(rot[:, 1, h0:h1, 0:H2], heads_a[c][:, h0:h1, H2:HD],
                                        bc(rope_s[:, a, c, 0:H2], 1, n), ALU.mult)
                        then(v.tensor_tensor(rot[:, 1, h0:h1, H2:HD], heads_a[c][:, h0:h1, 0:H2],
                                             bc(rope_s[:, a, c, H2:HD], 1, n), ALU.mult))
                    v.tensor_tensor(heads_a[c][:, 0:HQ, :], rot[:, 0, 0:HQ, :], rot[:, 1, 0:HQ, :], ALU.add)
                    for half in (0, 1):
                        ins = v.tensor_tensor(k_dup[:, c, :, half, :], rot[:, 0, HQ:SWA_H, :], rot[:, 1, HQ:SWA_H, :],
                                              ALU.add)
                    ins.then_inc(qk_ready, 1)
                if g == G_GATE + 5:
                    dve.wait_ge(fl_ln, 1)
                    for at in range(0, P, 32):
                        ins = v.scalar_tensor_tensor(out=lf[:, :, at:at + HF], in0=fl[:, :, :], scalar=0.0,
                                                     in1=fl_a[:, :, :], op0=ALU.min, op1=ALU.subtract)
                    ins.then_inc(lf_ready, 1)
            dve.wait_ge(c_hi_ready, 1)
            for r in (32, 96):
                ins = v.scalar_tensor_tensor(out=c_rows[r:r + 32, :], in0=ps[r:r + 32, 7, :], scalar=-1.0 / SCALE,
                                             in1=c_hi[r:r + 32, :].bitcast(F32), op0=ALU.mult, op1=ALU.subtract)
            ins.then_inc(c_ready, 1)
            for n in range(0, len(QKT), 2):
                s, j = QKT[n]
                dve.wait_ge(qkT_ps, n + 1)
                dst, src = (qaT, kaT, qfT, kfT)[s][:, j, :], ps[:, QKT_BANK[n % 4], :]
                scale = 1.0 if s < 2 else g_fx[:, s - 2:s - 1]
                v.tensor_scalar(dst, src, scale, None, ALU.mult).then_inc(qkT_out[0], 1)

            def finish_block(u):
                c, b = u // 2, u % 2
                dve.wait_ge(probs, 8 * u + 8)
                sums = den[:, 8 * u:8 * u + 8]
                if b == 0:
                    dve.wait_ge(snk_exp, c + 1)
                    then(v.tensor_tensor(sums, sums, snk[:, :], ALU.add))
                then(v.reciprocal(rden[:, 8 * u:8 * u + 8], sums))
                dve.wait_ge(pv_done, 8 * u + 8)
                v.tensor_tensor(o_tok[:, c, b * QW:(b + 1) * QW].rearrange("p (h d) -> p h d", d=HD),
                                ps[:, 6 + b, :].rearrange("p (h d) -> p h d", d=HD),
                                bc(rden[:, 8 * u:8 * u + 8], 2, HD), ALU.mult).then_inc(o_out, 1)

            for n in range(NU + 5):
                if n < NU:
                    c, b, h = units[n]
                    dve.wait_ge(scores, n + 1)
                    v.reduce_max(mx[:, n:n + 1], ps[:, n % 4, 0:width(n)], AX.X).then_inc(maxed, 1)
                if 2 <= n < NU + 2:
                    m = n - 2
                    dve.wait_ge(pT_ps, m + 1)
                    if m >= 2:
                        dve.wait_ge(pv_done, m - 1)
                    v.tensor_copy(pT_sb[:, m % 2, 0:width(m)], ps[:, 4 + m % 2, 0:width(m)]).then_inc(pT_ready, 1)
                if n < NU:
                    dve.wait_ge(maxed, n + 1)
                    if b == 0:
                        v.tensor_scalar(nb[:, n:n + 1], mx[:, n:n + 1], sink8[:, h:h + 1], -SCALE,
                                        ALU.max, ALU.mult).then_inc(shift, 1)
                    else:
                        v.tensor_scalar(nb[:, n:n + 1], mx[:, n:n + 1], -SCALE, None, ALU.mult).then_inc(shift, 1)
                    if b == 0 and h == 7:
                        dve.wait_ge(shift, n + 1)
                        v.tensor_tensor(snk[:, :], sink_bc[:, :], nb[:, n - 7:n + 1], ALU.add).then_inc(snk_in, 1)
                if n >= 12 and (n - 12) % 8 == 0:
                    finish_block((n - 12) // 8)
            for k in range(KD):
                dve.wait_ge(oT_hi, k + 1)
                v.tensor_tensor(oT_l[:, k, :], ps[:, k, :], oT_h[:, k, :].bitcast(F32), ALU.subtract).then_inc(oT_ready, 1)

            split_low(G_O + 1)

            def merge_low(j):
                dve.wait_ge(m_hi, j + 1)
                v.tensor_tensor(mT_l[:, j, :], merge_s[:, j % 2, :], mT_h[:, j, :].bitcast(F32),
                                ALU.subtract).then_inc(m_ready, 1)

            for g in range(G_O, G_OUT):
                if g > G_O:
                    split_low(g + 1)
                for d in (0, 1):
                    if d == 0:
                        dve.wait_ge(half_done, g - G_O + 1)
                    else:
                        dve.wait_ge(group_done, g + 1)
                    j, bank = 2 * (g - G_O) + d, (g - G_O) % 2 * 4 + 2 * d
                    if j >= 1:
                        dve.wait_ge(m_sum, j)
                    v.tensor_tensor(merge_t[:, 0, :], ps[:, bank, :], gates_T[:, j, :], ALU.mult)
                    v.tensor_tensor(merge_t[:, 1, :], ps[:, bank + 1, :], gates_T[:, KD + j, :], ALU.mult).then_inc(m_part, 1)
                    if j >= 1:
                        merge_low(j - 1)
                    dve.wait_ge(m_part, j + 1)
                    if j >= 2:
                        dve.wait_ge(m_ready, j - 1)
                    v.tensor_tensor(merge_s[:, j % 2, :], merge_t[:, 0, :], merge_t[:, 1, :], ALU.add).then_inc(m_sum, 1)
            merge_low(KD - 1)

            def keep_even(k):
                dve.wait_ge(h2T_ps, k + 1)
                v.tensor_scalar(h2T[:, k, :], ps[:, 4, :], vcol[:, 8 + k:9 + k], None, ALU.mult).then_inc(h2T_out[0], 1)

            for m in range(N_OUT):
                if m + 1 < N_OUT:
                    split_low(G_OUT + m + 1)
                dve.wait_ge(group_done, G_OUT + m + 1)
                s, b0 = slice(m * GW, (m + 1) * GW), m % 2 * 2
                v.tensor_tensor(x_tok[:, :, s], x_tok[:, :, s],
                                ps[:, b0:b0 + 2, :].rearrange("p b (c n) -> p (b c) n", c=2), ALU.add).then_inc(x1_ready, 1)
                if m >= 1:
                    keep_even(2 * m - 2)
            keep_even(KD - 2)
            dve.wait_ge(x1_squared, N_OUT)
            v.tensor_reduce(ssq[:, 1, :], ssq_g[:, :, :].rearrange("p m c -> p c m"), AX.X, ALU.add).then_inc(x1_sum, 1)
            dve.wait_ge(x1_sum, 1)
            v.tensor_scalar(ssq[:, 1, :], ssq[:, 1, :], 1.0 / D, EPS, ALU.mult, ALU.add).then_inc(var_ready, 1)

            dve.wait_ge(rstd_ready, 2)
            dve.wait_ge(logits_ps, 1)
            for c in range(NB):
                ins = v.scalar_tensor_tensor(out=lg[:, c, :], in0=ps[:, 6, c * E:(c + 1) * E], scalar=rstd[:, 1, c:c + 1],
                                             in1=brt[:, :], op0=ALU.mult, op1=ALU.add)
            then(ins)
            for c in range(NB):
                ins = v.max(top8[:, c, :], lg[:, c, :])
            then(ins)
            least = bc(top8[:, :, TOP_K - 1], 2, E)
            v.tensor_tensor(r_ex[:, :, :], lg[:, :, :], bc(top8[:, :, 0], 2, E), ALU.subtract).then_inc(r_shifted, 1)
            v.tensor_tensor(r_eq[:, :, :], lg[:, :, :], least, ALU.is_equal)
            then(v.tensor_tensor(r_gt[:, :, :], lg[:, :, :], least, ALU.is_gt))
            v.tensor_reduce(need[:, :], r_gt[:, :, :], AX.X, ALU.add)
            for c in range(NB):
                ins = v.tensor_tensor_scan(r_in[:, c, :], r_eq[:, c, :], zeros[:, 0:E], 0.0, ALU.add, ALU.add)
            then(ins)
            then(v.tensor_scalar(need[:, :], need[:, :], -1.0, float(TOP_K), ALU.mult, ALU.add))
            then(v.tensor_tensor(r_in[:, :, :], r_in[:, :, :], bc(need[:, :], 2, E), ALU.is_le))
            then(v.tensor_tensor(r_eq[:, :, :], r_eq[:, :, :], r_in[:, :, :], ALU.mult))
            then(v.tensor_tensor(r_eq[:, :, :], r_eq[:, :, :], r_gt[:, :, :], ALU.add))
            v.tensor_copy(sel_b[:, :, :], r_eq[:, :, :]).then_inc(picked, 1)
            dve.wait_ge(r_exp, 1)
            then(v.tensor_tensor(r_ex[:, :, :], r_ex[:, :, :], r_eq[:, :, :], ALU.mult))
            then(v.tensor_reduce(zsum[:, :], r_ex[:, :, :], AX.X, ALU.add))
            then(v.reciprocal(zsum[:, :], zsum[:, :]))
            v.tensor_tensor(r_gt[:, :, :], r_ex[:, :, :], bc(zsum[:, :], 2, E), ALU.mult).then_inc(gates_ready, 1)
            v.tensor_scalar(row_tab[:, :, :, 0], bc(zeros[:, :], 1, NB), tok_f[:, 0:1], None, ALU.add)
            for c in range(NB):
                v.memset(row_tab[:, c, :, 1], P * c - BIG)

            def split_gates(s, gates, rest):
                then(v.tensor_copy(row_tab[:, :, s, 2], gates))
                then(v.tensor_tensor(rest, gates, row_tab[:, :, s, 2], ALU.subtract))
                then(v.tensor_copy(row_tab[:, :, s, 3], rest))
                v.tensor_tensor(row_tab[:, :, s, 4], rest, row_tab[:, :, s, 3], ALU.subtract)

            dve.wait_ge(gates_ready, 1)
            split_gates(slice(0, E), r_gt[:, :, :], r_ex[:, :, :])
            v.memset(row_tab[:, :, ITEMS - 2:ITEMS, 2:5], 0.0)
            v.memset(slot_tab[:, :, ITEMS - 2:ITEMS], -1.0)
            dve.wait_ge(place_ps, 1)
            v.tensor_copy(cnt[:, :], ps[:, 4, 0:E])
            then(v.scalar_tensor_tensor(out=r_in[:, :, :], in0=ps[:, 7, 0:NB * E].rearrange("p (c e) -> p c e", c=NB),
                                        scalar=1.0, in1=r_eq[:, :, :], op0=ALU.add, op1=ALU.mult))
            then(v.tensor_scalar(slot_tab[:, :, 0:E], r_in[:, :, :], -1.0, None, ALU.add))

            def pick(i, first=False):
                if not first:
                    dve.wait_ge(list_ps, i)
                for c in range(NB):
                    ins = v.tensor_scalar(sel[:, c, :], iota_f[:, 0:SLOTS],
                                          slot_tab[:, c, i:i + 1] if isinstance(i, int) else slot_tab[:, c, bass.ds(i, 1)],
                                          None, ALU.is_equal)
                ins.then_inc(sel_ready, 1)

            def index(i, first=False):
                col = slice(i, i + 1) if isinstance(i, int) else bass.ds(i, 1)
                dve.wait_ge(list_ps, i + 1)
                if not first:
                    dve.wait_ge(xg_in, i * 16)
                v.tensor_reduce(row_f[:, :], list_v[:, 0:2], AX.X, ALU.add).then_inc(row_sum, 1)
                v.tensor_reduce(gate_all[:, col], list_v[:, 2:5], AX.X, ALU.add)
                dve.wait_ge(row_sum, i + 1)
                v.tensor_scalar(idx_g[:, :], row_f[:, :], BIG, float(T - 1), ALU.add, ALU.min)
                v.tensor_scalar(idx_all[:, col], row_f[:, :], BIG, spare[0:SLOTS, :], ALU.add, ALU.min).then_inc(idx_ready, 1)

            def move_rows(i, first=False):
                dve.wait_ge(xT_ps, i + 1)
                if not first:
                    dve.wait_ge(gu_used[KD - 1], i)
                v.tensor_tensor(xT[:, :, :], xT_ps_v, bc(vcol[:, 8:8 + KD], 2, SLOTS), ALU.mult).then_inc(xT_ready, 1)

            def rows_low(n):
                dve.wait_ge(xT_hi, n)
                v.tensor_tensor(xT_l[:, :, :], xT[:, :, :], xT_h[:, :, :].bitcast(F32), ALU.subtract).then_inc(xT_split, 1)

            def gate_up_low(n, ks):
                for k in ks:
                    dve.wait_ge(gu_hi_done, n * KD + (k + 1))
                    v.tensor_tensor(gu_low(k), split_columns(gu_chunk(k)), gu_hi[:, k % 4].bitcast(F32),
                                    ALU.subtract).then_inc(gu_split, 1)

            def activate(i, e, first=False, ahead=True):
                at = bgu[:, e, :] if isinstance(e, int) else bgu[:, bass.ds(e, 1), :].rearrange("p a j -> p (a j)")
                if not first:
                    dve.wait_ge(a_ready, i)
                if first:
                    dve.wait_ge(gu_used[KD - 1], 1)
                else:
                    dve.wait_ge(gu_turned, i)
                v.tensor_tensor(act_g[:, :, :], gu_v[:, 0:KD], bc(at[:, 0:KD], 2, SLOTS), ALU.add).then_inc(g_biased, 1)
                v.tensor_tensor(act_u[:, :, :], gu_v[:, KD:2 * KD], bc(at[:, KD:2 * KD], 2, SLOTS), ALU.add).then_inc(gu_out, 1)
                if ahead:
                    rows_low(i + 1)
                dve.wait_ge(g_biased, i + 1)
                v.tensor_scalar(act_g[:, :, :], act_g[:, :, :], LIMIT, None, ALU.min).then_inc(g_ready, 1)
                dve.wait_ge(gu_out, i + 1)
                v.tensor_scalar(act_u[:, :, :], act_u[:, :, :], LIMIT, -LIMIT, ALU.min, ALU.max).then_inc(u_ready, 1)
                if ahead and not first:
                    gate_up_low(i + 1, range(4))
                dve.wait_ge(sig_ready, i + 1)
                v.tensor_tensor(act_g[:, :, :], act_g[:, :, :], act_s[:, :, :], ALU.mult).then_inc(gs_ready, 1)
                dve.wait_ge(gs_ready, i + 1)
                dve.wait_ge(u_ready, i + 1)
                if not first:
                    dve.wait_ge(dn_used[3], i)
                v.scalar_tensor_tensor(out=aT[:, :, :], in0=act_u[:, :, :], scalar=1.0, in1=act_g[:, :, :],
                                       op0=ALU.add, op1=ALU.mult).then_inc(a_whole, 1)
                if ahead:
                    dve.wait_ge(a_hi, i + 1)
                    v.tensor_tensor(aT_l[:, :, :], aT[:, :, :], aT_h[:, :, :].bitcast(F32),
                                    ALU.subtract).then_inc(a_ready, 1)

            def down_low(n, js=range(4)):
                for j in js:
                    dve.wait_ge(dn_hi, n * 4 + (j + 1))
                    v.tensor_tensor(wdn_l[:, j], wdn[:, j], wdn_h[:, j].bitcast(F32),
                                    ALU.subtract).then_inc(dn_lo, 1)

            def add_bias(c):
                for m in (2 * c, 2 * c + 1):
                    n0 = m % 2 * 512
                    dve.wait_ge(bdn_ps, m + 1)
                    v.tensor_tensor(x_tok[:, c, n0:n0 + 512], x_tok[:, c, n0:n0 + 512], ps[:, 4 + m % 2, :],
                                    ALU.add).then_inc(bdn_out, 1)

            pick(0, first=True)
            index(0, first=True)
            add_bias(0)
            move_rows(0, first=True)
            pick(1)
            then(v.tensor_scalar(ext[:, :], cnt[:, :], float(SLOTS), None, ALU.is_gt))
            for j in range(2, LEVELS + 1):
                then(v.scalar_tensor_tensor(out=ext[:, :], in0=cnt[:, :], scalar=float(SLOTS * j), in1=ext[:, :],
                                            op0=ALU.is_gt, op1=ALU.add))
            then(v.tensor_tensor_scan(ext_in[:, :], ext[:, :], zeros[:, 0:E], 0.0, ALU.add, ALU.add))
            v.tensor_tensor(ext_ex[:, :], ext_in[:, :], ext[:, :], ALU.subtract)
            number = iota_f[:, 0:MAX_EXTRA]
            then(v.tensor_tensor(onehot_t[:, :, :], bc(ext_in[:, :], 1, MAX_EXTRA), bc(number, 2, E), ALU.is_le))
            then(v.tensor_reduce(item_e[:, :], onehot_t[:, :, :], AX.X, ALU.add))
            then(v.memset(items_f[:, :], 0.0))
            v.tensor_tensor(onehot[:, :, :], bc(iota_f[:, 0:E], 1, MAX_EXTRA), bc(item_e[:, :], 2, E), ALU.is_equal)
            then(v.tensor_scalar(item_b[:, :], item_e[:, :], float(E - 1), None, ALU.min))
            v.tensor_copy(items_f[:, 0:E], iota_f[0:1, 0:E])
            v.tensor_copy(items_f[:, E:E + MAX_EXTRA], item_b[0:1, :])
            v.tensor_scalar(items_f[:, LAST_AT:LAST_AT + 1], ext_in[0:1, E - 1:E], float(E - 1), None, ALU.add)
            then(v.tensor_scalar(items_f[:, N_AT:N_AT + 1], ext_in[0:1, E - 1:E], float(E), None, ALU.add))
            v.tensor_copy(items[:, :], items_f[:, :]).then_inc(items_ready, 1)
            index(1)
            pick(2)
            then(v.tensor_tensor(onehot_t[:, :, :], onehot[:, :, :], bc(ext_ex[:, :], 1, MAX_EXTRA), ALU.mult))
            then(v.tensor_reduce(item_b[:, :], onehot_t[:, :, :], AX.X, ALU.add))
            then(v.tensor_tensor(item_b[:, :], number, item_b[:, :], ALU.subtract))
            then(v.tensor_scalar(item_b[:, :], item_b[:, :], float(SLOTS), float(SLOTS), ALU.mult, ALU.add))
            for c in range(NB):
                then(v.tensor_tensor(onehot_t[:, :, :], onehot[:, :, :], bc(r_gt[:, c, :], 1, MAX_EXTRA), ALU.mult))
                then(v.tensor_reduce(r_in[:, c, 0:MAX_EXTRA], onehot_t[:, :, :], AX.X, ALU.add))
                then(v.tensor_tensor(onehot_t[:, :, :], onehot[:, :, :], bc(slot_tab[:, c, 0:E], 1, MAX_EXTRA), ALU.mult))
                then(v.tensor_reduce(slot_tab[:, c, E:E + MAX_EXTRA], onehot_t[:, :, :], AX.X, ALU.add))
                then(v.tensor_tensor(slot_tab[:, c, E:E + MAX_EXTRA], slot_tab[:, c, E:E + MAX_EXTRA], item_b[:, :],
                                     ALU.subtract))
                if c + 1 < NB:
                    add_bias(c + 1)
                if c == 0:
                    index(2)
            split_gates(slice(E, E + MAX_EXTRA), r_in[:, :, 0:MAX_EXTRA], r_eq[:, :, 0:MAX_EXTRA])
            dve.sem_inc(gu_split, KD)
            dve.sem_inc(dn_lo, 4)
            gate_up_low(1, range(4))
            move_rows(1)
            activate(0, 0, first=True)
            dve.wait_ge(bdn_out, 8)
            v.memset(need[:, 0:1], 0.0).then_inc(y_ready, 1)

            def dve_item(i, ahead=True):
                e = dve.value_load(items[0:1, bass.ds(i, 1)], min_val=0, max_val=E - 1)
                pick(i + 2)
                for j in range(4):
                    down_low(i, (j,))
                    gate_up_low(i, (4 + j,))
                    if j == 1:
                        index(i + 2)
                move_rows(i + 1)
                activate(i, e, ahead=ahead)

            last = dve.value_load(items[0:1, LAST_AT:LAST_AT + 1], min_val=E - 1, max_val=E + MAX_EXTRA - 1)
            with dve.Fori(1, last) as i:
                dve_item(i)
            dve_item(last, ahead=False)

        @block.tensor
        def _(pe):
            pe.wait_ge(ident_done, 1)
            pe.wait_ge(rows_in, 64)
            pe.transpose(ps[:, 6, 0:32], vec_rows[:, :], ident[0:32, 0:32]).then_inc(rows_ps, 1)
            for j in range(2 * KD):
                ins = pe.transpose(ps[:, 7, j * E:(j + 1) * E], bgu_rows[:, j * P:(j + 1) * P], ident[0:E, 0:E])
            ins.then_inc(rows_ps, 1)

            for k in range(KD):
                if k >= 4:
                    pe.wait_ge(hT_ready, k - 3)
                for c in range(NB):
                    if k == 0:
                        pe.wait_ge(hn_ready, c + 1)
                    ins = pe.transpose(ps[:, k % 4, c * P:(c + 1) * P], hn_tok[:, c, k * P:(k + 1) * P], ident[:, :])
                ins.then_inc(hT_ps, 1)

            def rows_times_group(dst, xh, xl, wh, wl, waits):
                n = xh.shape[1]
                for k in range(n):
                    if waits:
                        pe.wait_ge(m_ready, k + 1)
                    pe.matmul(dst, xh[:, k], wh[:, k], start=(k == 0), stop=False)
                    pe.matmul(dst, xh[:, k], wl[:, k], start=False, stop=False)
                    ins = pe.matmul(dst, xl[:, k], wh[:, k], start=False, stop=(k == n - 1))
                return ins

            def group_times_rows(dst, wh, wl, xh, xl):
                n = wh.shape[1]
                for k in range(n):
                    pe.matmul(dst, wh[:, k], xh[:, k], start=(k == 0), stop=False)
                    pe.matmul(dst, wh[:, k], xl[:, k], start=False, stop=False)
                    ins = pe.matmul(dst, wl[:, k], xh[:, k], start=False, stop=(k == n - 1))
                return ins

            def token_group(bank, buffer, xh, xl, waits=False):
                for c in range(NB):
                    dst = ps[:, bank + c // 2, c % 2 * GW:(c % 2 + 1) * GW]
                    s = slice(c * P, (c + 1) * P)
                    ins = rows_times_group(dst, xh[:, :, s], xl[:, :, s], st_h[:, buffer], st_l[:, buffer],
                                           waits and c == 0)
                ins.then_inc(group_done, 1)

            pe.wait_ge(hT_ready, KD)
            for g in (0, 1):
                pe.wait_ge(split_lo, g + 1)
                token_group(2 * g, g, hT_h, hT_l)
            with pe.Fori(0, G_GATE // 2 - 1) as pair:
                for b in (0, 1):
                    pe.wait_ge(split_lo, pair * 2 + (b + 3))
                    pe.wait_ge(group_out, pair * 2 + (b + 1))
                    token_group(2 * b, b, hT_h, hT_l)
            pe.wait_ge(wfl_ready, 1)
            pe.wait_ge(vcol_ready, 1)
            for k in range(KD):
                pe.matmul(ps[0:64, 6, :], wfl_hl[:, k, :], hT_h[:, k, :], start=(k == 0), stop=False)
                ins = pe.matmul(ps[0:64, 6, :], wfl_hl[:, k, :], hT_l[:, k, :], start=False, stop=(k == KD - 1))
            ins.then_inc(flT_ps, 1)
            pe.wait_ge(split_lo, G_GATE)
            pe.wait_ge(group_out, G_GATE - 2)
            token_group(0, 0, hT_h, hT_l)
            pe.wait_ge(flT_ready, 1)
            for c in range(NB):
                ins = pe.matmul(ps[:, 6, c * HF:(c + 1) * HF], flT[:, c * P:(c + 1) * P], c_pick[0:64, :],
                                start=True, stop=True)
            ins.then_inc(fl_ps, 1)

            def gate_group(b):
                for d in (0, 1):
                    s = slice(d * P, (d + 1) * P)
                    ins = group_times_rows(ps[:, 2 * b + d, :], st_h[:, b, :, s], st_l[:, b, :, s], hT_h, hT_l)
                ins.then_inc(group_done, 1)

            with pe.Fori(0, N_GATE // 2 - 1) as pair:
                for b in (0, 1):
                    pe.wait_ge(split_lo, pair * 2 + (G_GATE + b + 1))
                    pe.wait_ge(group_out, pair * 2 + (G_GATE + b - 1))
                    gate_group((G_GATE + b) % 2)
            pe.wait_ge(split_lo, G_O - 1)
            pe.wait_ge(group_out, G_O - 3)
            gate_group((G_O - 2) % 2)

            pe.wait_ge(lf_ready, 1)
            pe.wait_ge(bgu_ready, 1)
            for c in range(NB):
                ins = pe.matmul(ps[:, 7, c * P:T], lf[:, c, :], upto[:, 0:T - c * P], start=(c == 0), stop=(c == NB - 1))
            ins.then_inc(c_ps, 1)
            pe.wait_ge(split_lo, G_O)
            pe.wait_ge(group_out, G_O - 2)
            gate_group((G_O - 1) % 2)

            pe.wait_ge(qk_ready, NB)
            pe.wait_ge(group_out, G_O - 1)
            for n, (s, j) in enumerate(QKT):
                if n >= 4:
                    pe.wait_ge(qkT_out[n % 2], n // 2 - 1)
                for c in range(NB):
                    c0 = (0, None, QF, KF)[s]
                    src = k_dup[:, c, j].rearrange("p a d -> p (a d)") if s == 1 else tok[:, c, c0 + j * P:c0 + (j + 1) * P]
                    ins = pe.transpose(ps[:, QKT_BANK[n % 4], c * P:(c + 1) * P], src, ident[:, :])
                ins.then_inc(qkT_ps, 1)

            def unit_scores(n):
                c, fox, h = units[n]
                w, bank = width(n), n % 4
                if n >= 4:
                    pe.wait_ge(probs, n - 3)
                rows = slice(h % 2 * HD, (h % 2 + 1) * HD)
                q = (qfT if fox else qaT)[rows, h // 2, c * P:(c + 1) * P]
                k0 = (c + 1) * P - w
                kv = kfT[rows, h // 2, k0:k0 + w] if fox else kaT[rows, h // (HQ // KV), k0:k0 + w]
                pe.matmul(ps[:, bank, 0:w], q, kv, start=True, stop=False)
                if fox:
                    pe.matmul(ps[:, bank, 0:w], c_pick_r[rows, h:h + 1].broadcast_to([HD, P]), c_rows[rows, 0:w],
                              start=False, stop=False)
                    ins = pe.matmul(ps[:, bank, w - P:w], ident_b[:, :], mask_b[:, 1, :], start=False, stop=True)
                else:
                    m = mask_b[:, :, :].rearrange("p a k -> p (a k)")[:, 2 * P - w:2 * P]
                    ins = pe.matmul(ps[:, bank, 0:w], ident_b[:, :], m, start=False, stop=True)
                ins.then_inc(scores, 1)

            def unit_transposes(n):
                pe.wait_ge(probs, n + 1)
                if n >= 2:
                    pe.wait_ge(pT_ready, n - 1)
                for kb in range(width(n) // P):
                    ins = pe.transpose(ps[:, 4 + n % 2, kb * P:(kb + 1) * P], p_sb[:, n % 3, kb * P:(kb + 1) * P], ident[:, :])
                ins.then_inc(pT_ps, 1)

            def unit_values(n):
                c, fox, h = units[n]
                u, nk = n // 8, width(n) // P
                pe.wait_ge(pT_ready, n + 1)
                if n % 8 == 0 and u >= 2:
                    pe.wait_ge(o_out, u - 1)
                v0 = VF + h * HD if fox else VA + h // (HQ // KV) * HD
                for kb in range(nk):
                    ins = pe.matmul(ps[:, 6 + fox, h * HD:(h + 1) * HD], pT_sb[:, n % 2, kb * P:(kb + 1) * P],
                                    tok[:, c + 1 - nk + kb, v0:v0 + HD], start=(kb == 0), stop=(kb == nk - 1))
                ins.then_inc(pv_done, 1)

            pe.wait_ge(c_ready, 1)
            pe.wait_ge(group_out, G_O)
            pe.wait_ge(qkT_out[0], (len(QKT) + 1) // 2)
            pe.wait_ge(qkT_out[1], len(QKT) // 2)
            for n in range(NU + 3):
                if n < NU:
                    unit_scores(n)
                if 2 <= n < NU + 2:
                    unit_transposes(n - 2)
                if n >= 3:
                    unit_values(n - 3)

            for k in range(KD):
                if k % 4 == 0:
                    pe.wait_ge(o_out, 2 * NB - 1 + k // 4)
                for c in range(NB):
                    ins = pe.transpose(ps[:, k, c * P:(c + 1) * P], o_tok[:, c, k * P:(k + 1) * P], ident[:, :])
                ins.then_inc(oT_ps, 1)
            for g in range(G_O, G_OUT):
                pe.wait_ge(split_lo, g + 1)
                if g >= G_O + 2:
                    pe.wait_ge(m_sum, 2 * (g - G_O - 1))
                for d in (0, 1):
                    s = slice(d * P, (d + 1) * P)
                    for branch in (0, 1):
                        kk = slice(4 * branch, 4 * branch + 4)
                        if g == G_O and d == 0:
                            pe.wait_ge(oT_ready, 4 * branch + 4)
                        ins = group_times_rows(ps[:, (g - G_O) % 2 * 4 + 2 * d + branch, :], st_h[:, g % 2, kk, s],
                                               st_l[:, g % 2, kk, s], oT_h[:, kk], oT_l[:, kk])
                    ins.then_inc(group_done if d else half_done, 1)

            def turn_x1(m):
                pe.wait_ge(x1_ready, m + 1)
                for k in (2 * m, 2 * m + 1):
                    if k >= 2:
                        pe.wait_ge(h2T_out[k % 2], k // 2)
                    for c in range(NB):
                        ins = pe.transpose(ps[:, 4 + k % 2, c * P:(c + 1) * P], x_tok[:, c, k * P:(k + 1) * P], ident[:, :])
                    ins.then_inc(h2T_ps, 1)

            def route(m):
                for k in (2 * m, 2 * m + 1):
                    pe.wait_ge(h2T_out[k % 2], k // 2 + 1)
                    for c in range(NB):
                        ins_logits[0] = pe.matmul(ps[:, 6, c * E:(c + 1) * E], h2T[:, k, c * P:(c + 1) * P], w_rt[:, k, :],
                                                  start=(k == 0 and c == 0), stop=(k == KD - 1), skip_group_check=True)

            ins_logits = [None]
            for g in range(G_OUT, G_END):
                pe.wait_ge(split_lo, g + 1)
                if g >= G_OUT + 2:
                    pe.wait_ge(x1_ready, g - G_OUT - 1)
                token_group((g - G_OUT) % 2 * 2, g % 2, mT_h, mT_l, waits=(g == G_OUT))
                if g > G_OUT:
                    turn_x1(g - 1 - G_OUT)
                if g > G_OUT + 1:
                    route(g - 2 - G_OUT)
            turn_x1(N_OUT - 1)
            route(N_OUT - 2)
            route(N_OUT - 1)
            ins_logits[0].then_inc(logits_ps, 1)
            pe.wait_ge(picked, 1)
            for c in range(NB):
                pe.matmul(ps[:, 4, 0:E], ones_b[:, :], sel_b[:, c, :], start=(c == 0), stop=(c == NB - 1))
            for c in range(NB):
                for c1 in range(c + 1):
                    ins = pe.matmul(ps[:, 7, c * E:(c + 1) * E], (before_b if c1 == c else ones_b)[:, :], sel_b[:, c1, :],
                                    start=(c1 == 0), stop=(c1 == c))
            ins.then_inc(place_ps, 1)
            pe.wait_ge(gates_ready, 1)
            pe.transpose(ps[:, 5, 0:P], r_gt[:, :, :].rearrange("p c e -> p (c e)"), ident[:, :]).then_inc(gateT_ps, 1)

            def lists(i, first=False):
                pe.wait_ge(sel_ready, i + 1)
                if not first:
                    pe.wait_ge(idx_ready, i)
                for c in range(NB):
                    rhs = row_tab[:, c, i, :] if isinstance(i, int) else \
                        row_tab[:, c, bass.ds(i, 1), :].rearrange("p a t -> p (a t)")
                    ins = pe.matmul(list_v, sel[:, c, :], rhs, start=(c == 0), stop=(c == NB - 1))
                ins.then_inc(list_ps, 1)

            def turn_rows(i, first=False):
                pe.wait_ge(xg_in, i * 16 + 16)
                if not first:
                    pe.wait_ge(xT_ready, i)
                    pe.wait_ge(idx_ready, i + 2)
                for k in range(KD):
                    ins = pe.transpose(xT_ps_v[:, k], xg[:, k * P:(k + 1) * P], ident[0:SLOTS, 0:SLOTS])
                ins.then_inc(xT_ps, 1)

            def bias_rows(c):
                pe.wait_ge(gateT_ready, 1)
                pe.wait_ge(b_dn_in, 16 * NB)
                for m in (2 * c, 2 * c + 1):
                    if m >= 2:
                        pe.wait_ge(bdn_out, m - 1)
                    pe.matmul(ps[:, 4 + m % 2, :], gateT[c * E:(c + 1) * E, :],
                              b_dn[c * E:(c + 1) * E, m % 2 * 512:(m % 2 + 1) * 512], start=True, stop=True).then_inc(bdn_ps, 1)

            def gate_up(i, first=False):
                if first:
                    pe.wait_ge(xT_ready, 1)
                else:
                    pe.wait_ge(xT_split, i)
                    pe.wait_ge(gu_out, i)
                for k in range(KD):
                    if first:
                        pe.wait_ge(gu_in[k], 16)
                    else:
                        pe.wait_ge(gu_split, i * KD + (k + 1))
                        for half in (0, 1):
                            dst, w_h, w_l = ps[0:SLOTS, 1 + 2 * half, :], gu_hi[:, k % 4, half, :], gu_low(k)[:, half, :]
                            pe.matmul(dst, xT_h[:, k, :], w_h, start=(k == 0), stop=False)
                            pe.matmul(dst, xT_h[:, k, :], w_l, start=False, stop=False)
                            ins = pe.matmul(dst, xT_l[:, k, :], w_h, start=False, stop=(k == KD - 1))
                        if k == KD - 1:
                            ins.then_inc(rows_done, 1)
                    for f in range(2 * KD) if first else (*range(0, 4), *range(8, 12)):
                        ins = pe.matmul(gu_v[:, f], gu_chunk(k)[:, f * P:(f + 1) * P], xT[:, k, :],
                                        start=(k == 0 and f % 4 == 0), stop=(k == KD - 1), skip_group_check=True)
                    ins.then_inc(gu_used[k], 1)
                    if k == 1:
                        lists(1 if first else i + 2)
                    if first and k == 3:
                        lists(2)
                    if first and 2 <= k < 1 + NB:
                        bias_rows(k - 1)

            def turn_gate_up(i):
                for half in (0, 1):
                    pe.wait_ge(rows_kept, i * 2)
                    for j in range(4):
                        ins = pe.transpose(gu_v[:, 8 * half + 4 + j], gu_tok[:, half, j * P:(j + 1) * P],
                                           ident[0:SLOTS, 0:SLOTS])
                ins.then_inc(gu_turned, 1)

            def last_down(n):
                pe.wait_ge(a_whole, n)
                pe.wait_ge(y_ready, n)
                for f in range(KD):
                    pe.wait_ge(last_dn_in[f // 2], 16)
                    for half in (0, 1):
                        w = gu_head[:, f // 2, f % 2 * D + half * 512:f % 2 * D + (half + 1) * 512]
                        ins = pe.matmul(ps[0:SLOTS, 4 + half, :], aT[:, f, :], w, start=(f == 0), stop=(f == KD - 1))
                ins.then_inc(dn_used[3], 1)

            def down(n):
                pe.wait_ge(a_ready, n)
                pe.wait_ge(y_ready, n)
                for j in range(4):
                    pe.wait_ge(dn_lo, n * 4 + (j + 1))
                    for k in (0, 1):
                        f = 2 * j + k
                        a_h, a_l = aT_h[:, f, :], aT_l[:, f, :]
                        for half in (0, 1):
                            s = slice(half * 512, (half + 1) * 512)
                            w_h, w_l = wdn_h[:, j, k, s], wdn_l[:, j, k, s]
                            pe.matmul(ps[0:SLOTS, 4 + half, :], a_h, w_h, start=(f == 0), stop=False)
                            pe.matmul(ps[0:SLOTS, 4 + half, :], a_h, w_l, start=False, stop=False)
                            ins = pe.matmul(ps[0:SLOTS, 4 + half, :], a_l, w_h, start=False, stop=(f == KD - 1))
                    ins.then_inc(dn_used[j], 1)

            lists(0, first=True)
            bias_rows(0)
            turn_rows(0, first=True)
            gate_up(0, first=True)
            turn_rows(1)
            pe.wait_ge(items_ready, 1)
            n_items = pe.value_load(items[0:1, N_AT:N_AT + 1], min_val=E, max_val=E + MAX_EXTRA)
            with pe.Fori(1, n_items) as i:
                gate_up(i)
                turn_rows(i + 1)
                turn_gate_up(i)
                down(i)
            last_down(n_items)


_INS = ["x", "positions", "norm1_g", "w_in", "b_forget", "b_gate", "q_norm_swa", "k_norm_swa", "sinks",
        "q_norm_fox", "k_norm_fox", "w_o_swa", "w_o_fox", "w_out", "norm2_g", "w_router", "b_router",
        "w_gate_up", "b_gate_up", "w_down", "b_down"]


def kernel(**inputs):
    import numpy as _np
    import concourse.bacc as _bacc
    from concourse.bass_utils import run_bass_kernel_spmd as _run

    nc = _bacc.Bacc("TRN2", target_bir_lowering=False, num_devices=1)
    arrays, args = {}, []
    for name in _INS:
        a = _np.ascontiguousarray(inputs[name])
        arrays[f"in_{name}_dram"] = a
        args.append(nc.dram_tensor(f"in_{name}_dram", a.shape, mybir.dt.from_np(a.dtype), kind="ExternalInput").ap())
    args.append(nc.dram_tensor("out_0_dram", inputs["x"].shape, F32, kind="ExternalOutput").ap())
    hybrid_block(nc, *args)
    r = _run(nc, [arrays], core_ids=[0])
    return r.results[0]["out_0_dram"]
```
